# Optimizing a Trainium2 kernel written in Bass

```python
import jax, jax.numpy as jnp
from jax import lax
import numpy as np
import math

D_MODEL = 1024
BATCH = 1
SEQ = 256
DEPTH = 1

D_MIX = D_MODEL
GDN_HEADS = 4
GDN_DK = 128
GDN_DV = 128
MLSTM_HEADS = 4
MLSTM_DK = 128
MLSTM_DV = 128
N_DIR = 2
CONV_K = 5
CHUNK = 64
PEER_HEADS = 8
PEER_NKEYS = 128
PEER_N = PEER_NKEYS * PEER_NKEYS
PEER_DKEY = 256
PEER_TOPK = 16
PEER_BLOCK = 128
EPS = 1e-6

GDN_QK = GDN_HEADS * GDN_DK
GDN_V = GDN_HEADS * GDN_DV
ML_QK = MLSTM_HEADS * MLSTM_DK
ML_V = MLSTM_HEADS * MLSTM_DV
SPLIT_SIZES = (GDN_QK, GDN_QK, GDN_V, GDN_V, N_DIR * GDN_HEADS, N_DIR * GDN_HEADS,
               ML_QK, ML_QK, ML_V, ML_V, N_DIR * MLSTM_HEADS, N_DIR * MLSTM_HEADS)
D_IN = sum(SPLIT_SIZES)


def _rmsnorm(x, g):
    x32 = x.astype(jnp.float32)
    y = x32 * lax.rsqrt(jnp.mean(x32 * x32, axis=-1, keepdims=True) + EPS)
    return (y * g.astype(jnp.float32)).astype(x.dtype)

def _l2norm(x):
    return x * lax.rsqrt(jnp.sum(x * x, axis=-1, keepdims=True) + EPS)

def _to_heads(x, n_heads):
    b, s, _ = x.shape
    return x.astype(jnp.float32).reshape(b, s, n_heads, -1).transpose(0, 2, 1, 3)

def _chunk(x):
    b, h, s = x.shape[:3]
    return x.reshape(b, h, s // CHUNK, CHUNK, *x.shape[3:])

def _flip(x):
    return jnp.flip(x, axis=2)

def _conv_centred(x, w):
    c = x.shape[-1]
    rhs = w.astype(jnp.float32).T[:, None, :]
    return lax.conv_general_dilated(x, rhs, window_strides=(1,),
                                    padding=[(CONV_K // 2, CONV_K // 2)],
                                    dimension_numbers=("NWC", "WIO", "NWC"),
                                    feature_group_count=c)

def _gated_delta_rule(q, k, v, g, beta):
    b_, h_, s_, dk = q.shape
    dv = v.shape[-1]
    q, k, v, g, beta = (_chunk(a) for a in (q, k, v, g, beta))
    g = jnp.cumsum(g, axis=-1)
    incl = jnp.tril(jnp.ones((CHUNK, CHUNK), dtype=bool))
    strict = jnp.tril(jnp.ones((CHUNK, CHUNK), dtype=bool), k=-1)
    decay = jnp.exp(jnp.where(incl, g[..., :, None] - g[..., None, :], -jnp.inf))
    k_beta = k * beta[..., None]
    a_mat = jnp.where(strict, jnp.einsum("bhncd,bhnsd->bhncs", k_beta, k) * decay, 0.0)
    eye = jnp.eye(CHUNK, dtype=q.dtype)
    t_mat = lax.linalg.triangular_solve(eye + a_mat, jnp.broadcast_to(eye, a_mat.shape),
                                        left_side=True, lower=True)
    u = jnp.einsum("bhncs,bhnse->bhnce", t_mat, v * beta[..., None])
    w = jnp.einsum("bhncs,bhnsd->bhncd", t_mat, k_beta * jnp.exp(g)[..., None])
    qk = jnp.where(incl, jnp.einsum("bhncd,bhnsd->bhncs", q, k) * decay, 0.0)
    q_dec = q * jnp.exp(g)[..., None]
    k_dec = k * jnp.exp(g[..., -1:] - g)[..., None]
    g_tot = jnp.exp(g[..., -1])

    def step(state, inp):
        u_c, w_c, qk_c, qd_c, kd_c, gt_c = inp
        v_new = u_c - jnp.einsum("bhcd,bhde->bhce", w_c, state)
        o_c = (jnp.einsum("bhcd,bhde->bhce", qd_c, state)
               + jnp.einsum("bhcs,bhse->bhce", qk_c, v_new))
        state = state * gt_c[..., None, None] + jnp.einsum("bhcd,bhce->bhde", kd_c, v_new)
        return state, o_c

    xs = tuple(jnp.moveaxis(a, 2, 0) for a in (u, w, qk, q_dec, k_dec, g_tot))
    _, o = lax.scan(step, jnp.zeros((b_, h_, dk, dv), q.dtype), xs)
    return jnp.moveaxis(o, 0, 2).reshape(b_, h_, s_, dv)

def _mlstm(q, k, v, i_pre, f_pre):
    b_, h_, s_, dk = q.shape
    dv = v.shape[-1]
    q, k, v, i_pre, f_pre = (_chunk(a) for a in (q, k, v, i_pre, f_pre))
    incl = jnp.tril(jnp.ones((CHUNK, CHUNK), dtype=bool))
    bcum = jnp.cumsum(jax.nn.log_sigmoid(f_pre), axis=-1)
    d_log = jnp.where(incl, bcum[..., :, None] - bcum[..., None, :] + i_pre[..., None, :], -jnp.inf)
    m_intra = jnp.max(d_log, axis=-1)
    p = jnp.exp(d_log - m_intra[..., None]) * jnp.einsum("bhncd,bhnsd->bhncs", q, k)
    num_intra = jnp.einsum("bhncs,bhnse->bhnce", p, v)
    den_intra = jnp.sum(p, axis=-1)
    b_last = bcum[..., -1]
    w_log = b_last[..., None] - bcum + i_pre
    m_w = jnp.max(w_log, axis=-1)
    wgt = jnp.exp(w_log - m_w[..., None])
    dc = jnp.einsum("bhnc,bhncd,bhnce->bhnde", wgt, k, v)
    dn = jnp.einsum("bhnc,bhncd->bhnd", wgt, k)

    def step(carry, inp):
        c_st, n_st, m_st = carry
        q_c, b_c, mi_c, num_c, den_c, bl_c, mw_c, dc_c, dn_c = inp
        inter_log = b_c + m_st[..., None]
        m_t = jnp.maximum(inter_log, mi_c)
        s_inter = jnp.exp(inter_log - m_t)
        s_intra = jnp.exp(mi_c - m_t)
        num = (s_inter[..., None] * jnp.einsum("bhcd,bhde->bhce", q_c, c_st)
               + s_intra[..., None] * num_c)
        den = s_inter * jnp.einsum("bhcd,bhd->bhc", q_c, n_st) + s_intra * den_c
        h = num / jnp.maximum(jnp.abs(den), jnp.exp(-m_t))[..., None]
        m_new = jnp.maximum(bl_c + m_st, mw_c)
        s_old = jnp.exp(bl_c + m_st - m_new)
        s_new = jnp.exp(mw_c - m_new)
        c_st = s_old[..., None, None] * c_st + s_new[..., None, None] * dc_c
        n_st = s_old[..., None] * n_st + s_new[..., None] * dn_c
        return (c_st, n_st, m_new), h

    xs = tuple(jnp.moveaxis(a, 2, 0) for a in
               (q, bcum, m_intra, num_intra, den_intra, b_last, m_w, dc, dn))
    init = (jnp.zeros((b_, h_, dk, dv), q.dtype), jnp.zeros((b_, h_, dk), q.dtype),
            jnp.zeros((b_, h_), q.dtype))
    _, h = lax.scan(step, init, xs)
    return jnp.moveaxis(h, 0, 2).reshape(b_, h_, s_, dv)

def _gdn_group(q, k, v, z, a, bb, conv_w, a_log, dt_bias, norm_g):
    bsz, s, _ = q.shape
    qkv = jax.nn.silu(_conv_centred(jnp.concatenate([q, k, v], axis=-1).astype(jnp.float32), conv_w))
    qh = _l2norm(_to_heads(qkv[..., :GDN_QK], GDN_HEADS)) * (GDN_DK ** -0.5)
    kh = _l2norm(_to_heads(qkv[..., GDN_QK:2 * GDN_QK], GDN_HEADS))
    vh = _to_heads(qkv[..., 2 * GDN_QK:], GDN_HEADS)
    a = a.astype(jnp.float32).reshape(bsz, s, N_DIR, GDN_HEADS)
    bb = bb.astype(jnp.float32).reshape(bsz, s, N_DIR, GDN_HEADS)
    g = -jnp.exp(a_log.astype(jnp.float32)) * jax.nn.softplus(a + dt_bias.astype(jnp.float32))
    beta = jax.nn.sigmoid(bb)
    g = g.transpose(2, 0, 3, 1)
    beta = beta.transpose(2, 0, 3, 1)
    o_f = _gated_delta_rule(qh, kh, vh, g[0], beta[0])
    o_b = _flip(_gated_delta_rule(_flip(qh), _flip(kh), _flip(vh), _flip(g[1]), _flip(beta[1])))
    o = (o_f + o_b).transpose(0, 2, 1, 3)
    o = o * lax.rsqrt(jnp.mean(o * o, axis=-1, keepdims=True) + EPS) * norm_g.astype(jnp.float32)
    return o.reshape(bsz, s, GDN_V) * jax.nn.silu(z.astype(jnp.float32))

def _mlstm_group(q, k, v, o_gate, i_in, f_in, i_bias, f_bias, norm_g):
    bsz, s, _ = q.shape
    qh = _to_heads(q, MLSTM_HEADS)
    kh = _to_heads(k, MLSTM_HEADS) * (MLSTM_DK ** -0.5)
    vh = _to_heads(v, MLSTM_HEADS)
    i_pre = (i_in.astype(jnp.float32).reshape(bsz, s, N_DIR, MLSTM_HEADS)
             + i_bias.astype(jnp.float32)).transpose(2, 0, 3, 1)
    f_pre = (f_in.astype(jnp.float32).reshape(bsz, s, N_DIR, MLSTM_HEADS)
             + f_bias.astype(jnp.float32)).transpose(2, 0, 3, 1)
    h_f = _mlstm(qh, kh, vh, i_pre[0], f_pre[0])
    h_b = _flip(_mlstm(_flip(qh), _flip(kh), _flip(vh), _flip(i_pre[1]), _flip(f_pre[1])))
    h = (h_f + h_b).transpose(0, 2, 1, 3)
    h = (h * lax.rsqrt(jnp.mean(h * h, axis=-1, keepdims=True) + EPS)).reshape(bsz, s, ML_V)
    return h * norm_g.astype(jnp.float32) * jax.nn.sigmoid(o_gate.astype(jnp.float32))

def _peer(h, w_q, sub_keys, u_tab, v_tab):
    bsz, s, d = h.shape
    t = h.reshape(-1, d)
    n_tok = t.shape[0]
    qry = (t @ w_q).astype(jnp.float32).reshape(n_tok, PEER_HEADS, 2, PEER_DKEY // 2)
    scores = jnp.einsum("thpd,hpkd->thpk", qry, sub_keys.astype(jnp.float32))
    s_top, i_top = lax.top_k(scores, PEER_TOPK)
    cand = (s_top[:, :, 0, :, None] + s_top[:, :, 1, None, :]).reshape(n_tok, PEER_HEADS, -1)
    cand_idx = (i_top[:, :, 0, :, None] * PEER_NKEYS + i_top[:, :, 1, None, :]).reshape(n_tok, PEER_HEADS, -1)
    best, pos = lax.top_k(cand, PEER_TOPK)
    idx = jnp.take_along_axis(cand_idx, pos, axis=-1)
    gate = jax.nn.softmax(best, axis=-1)
    nb = n_tok // PEER_BLOCK

    def block_fn(args):
        tb, ib, gb = args
        u = u_tab[ib]
        act = jax.nn.gelu(jnp.einsum("td,thkd->thk", tb, u).astype(jnp.float32), approximate=False)
        vv = v_tab[ib]
        return jnp.einsum("thk,thkd->td", (gb * act).astype(vv.dtype), vv)

    out = lax.map(block_fn, (t.reshape(nb, PEER_BLOCK, d),
                             idx.reshape(nb, PEER_BLOCK, PEER_HEADS, PEER_TOPK),
                             gate.reshape(nb, PEER_BLOCK, PEER_HEADS, PEER_TOPK)))
    return out.reshape(bsz, s, d).astype(h.dtype)

def first_inputs(seed: int = 0) -> dict:
    key = jax.random.key(seed)
    ks = jax.random.split(key, 20)
    f32 = jnp.float32
    nrm = lambda k, shp, sc: jax.random.normal(k, shp, f32) * sc
    dt = jnp.exp(jax.random.uniform(ks[5], (DEPTH, N_DIR, GDN_HEADS), f32,
                                    np.log(1e-3).astype(np.float32), np.log(1e-1).astype(np.float32)))
    return {
        "x": nrm(ks[0], (BATCH, SEQ, D_MODEL), 1.0),
        "norm1_g": 1.0 + nrm(ks[1], (DEPTH, D_MODEL), 0.02),
        "w_in": nrm(ks[2], (DEPTH, D_MODEL, D_IN), D_MODEL ** -0.5),
        "conv_w": nrm(ks[3], (DEPTH, 2 * GDN_QK + GDN_V, CONV_K), CONV_K ** -0.5),
        "gdn_a_log": jnp.log(jax.random.uniform(ks[4], (DEPTH, N_DIR, GDN_HEADS), f32, 1.0, 16.0)),
        "gdn_dt_bias": jnp.log(jnp.expm1(dt)),
        "gdn_norm_g": 1.0 + nrm(ks[6], (DEPTH, GDN_DV), 0.02),
        "mlstm_i_bias": nrm(ks[7], (DEPTH, N_DIR, MLSTM_HEADS), 0.1),
        "mlstm_f_bias": jax.random.uniform(ks[8], (DEPTH, N_DIR, MLSTM_HEADS), f32, 3.0, 6.0),
        "mlstm_norm_g": 1.0 + nrm(ks[9], (DEPTH, ML_V), 0.02),
        "w_out": nrm(ks[10], (DEPTH, D_MIX, D_MODEL), D_MIX ** -0.5),
        "norm2_g": 1.0 + nrm(ks[11], (DEPTH, D_MODEL), 0.02),
        "peer_wq": nrm(ks[12], (DEPTH, D_MODEL, PEER_HEADS * PEER_DKEY), D_MODEL ** -0.5),
        "peer_keys": nrm(ks[13], (DEPTH, PEER_HEADS, 2, PEER_NKEYS, PEER_DKEY // 2), (PEER_DKEY // 2) ** -0.5),
        "peer_u": nrm(ks[14], (DEPTH, PEER_N, D_MODEL), D_MODEL ** -0.5),
        "peer_v": nrm(ks[15], (DEPTH, PEER_N, D_MODEL), PEER_HEADS ** -0.5),
        "normf_g": 1.0 + nrm(ks[16], (D_MODEL,), 0.02),
    }

def first_block(x, norm1_g, w_in, conv_w, gdn_a_log, gdn_dt_bias, gdn_norm_g, mlstm_i_bias,
              mlstm_f_bias, mlstm_norm_g, w_out, norm2_g, peer_wq, peer_keys, peer_u, peer_v,
              normf_g):
    offsets = [int(o) for o in np.cumsum(SPLIT_SIZES)[:-1]]
    for l in range(DEPTH):
        h = _rmsnorm(x, norm1_g[l])
        p = h @ w_in[l]
        (gq, gk, gv, gz, ga, gb, mq, mk, mv, mo, mi, mf) = jnp.split(p, offsets, axis=-1)
        y_a = _gdn_group(gq, gk, gv, gz, ga, gb, conv_w[l], gdn_a_log[l], gdn_dt_bias[l], gdn_norm_g[l])
        y_b = _mlstm_group(mq, mk, mv, mo, mi, mf, mlstm_i_bias[l], mlstm_f_bias[l], mlstm_norm_g[l])
        y = jnp.concatenate([y_a, y_b], axis=-1).astype(x.dtype)
        x = x + y @ w_out[l]
        h2 = _rmsnorm(x, norm2_g[l])
        x = x + _peer(h2, peer_wq[l], peer_keys[l], peer_u[l], peer_v[l])
    return _rmsnorm(x, normf_g)


DEPTH_2 = 2

CTX_LEN = 256
GRID_W = 64
N_MIXERS = 3
MIXER_POOL = 0
MIXER_ATTN = 1
MIXER_RET = 2
POOL_WINDOWS = (2, 4, 8, 16)
POOL_GROUP = D_MODEL // 4
ATTN_HEADS = 8
ATTN_KV_HEADS = 2
ATTN_HEAD_DIM = D_MODEL // ATTN_HEADS
ATTN_GROUP = ATTN_HEADS // ATTN_KV_HEADS
Q_BLOCK = 128
ROPE_THETA = 10000.0
RET_HEADS = 4
RET_DK = D_MODEL // RET_HEADS
RET_DV = 2 * D_MODEL // RET_HEADS
RET_CHUNK = 128
D_FF = 2816
CONV_WIDTH = 3


def _rmsnorm_2(x, gain):
    xf = x.astype(jnp.float32)
    y = xf * lax.rsqrt(jnp.mean(xf * xf, axis=-1, keepdims=True) + EPS)
    return (y * gain.astype(jnp.float32)).astype(x.dtype)

def _modulate(h, shift, scale):
    return h * (1.0 + scale) + shift

def _pool_mixer(h, w, b, scale):
    s = h.shape[1]
    hf = h.astype(jnp.float32)
    cs = jnp.concatenate([jnp.zeros_like(hf[:, :1]), jnp.cumsum(hf, axis=1)], axis=1)
    t = jnp.arange(s)
    outs = []
    for g, win in enumerate(POOL_WINDOWS):
        lo = jnp.clip(t - win // 2, 0, s)
        hi = jnp.clip(t + win // 2, 0, s)
        sl = slice(g * POOL_GROUP, (g + 1) * POOL_GROUP)
        csg = cs[..., sl]
        mean = (csg[:, hi] - csg[:, lo]) / (hi - lo).astype(jnp.float32)[None, :, None]
        outs.append((mean - hf[..., sl]).astype(h.dtype) @ w[g])
    return (jnp.concatenate(outs, axis=-1) + b) * scale

def _axial_angles(n_tokens):
    rows = n_tokens // GRID_W
    row = jnp.broadcast_to(jnp.arange(rows)[:, None], (rows, GRID_W)).reshape(-1).astype(jnp.float32)
    col = jnp.broadcast_to(jnp.arange(GRID_W)[None, :], (rows, GRID_W)).reshape(-1).astype(jnp.float32)
    axis_dim = ATTN_HEAD_DIM // 2
    inv = ROPE_THETA ** (-jnp.arange(0, axis_dim, 2, dtype=jnp.float32) / axis_dim)
    return row[:, None] * inv, col[:, None] * inv

def _rotate(xa, ang):
    x1, x2 = jnp.split(xa, 2, axis=-1)
    cos = jnp.cos(ang)[None, :, None, :]
    sin = jnp.sin(ang)[None, :, None, :]
    return jnp.concatenate([x1 * cos - x2 * sin, x1 * sin + x2 * cos], axis=-1)

def _apply_axial_rope(x, ang_row, ang_col):
    xr, xc = jnp.split(x.astype(jnp.float32), 2, axis=-1)
    return jnp.concatenate([_rotate(xr, ang_row), _rotate(xc, ang_col)], axis=-1).astype(x.dtype)

def _gqa(q, k, v):
    s = jnp.einsum('bqkgd,bskd->bkgqs', q, k).astype(jnp.float32) * (ATTN_HEAD_DIM ** -0.5)
    p = jax.nn.softmax(s, axis=-1).astype(v.dtype)
    return jnp.einsum('bkgqs,bskd->bqkgd', p, v)

def _attention_mixer(h_lat, h_ctx, w_qkv, q_gain, k_gain, w_o, need_ctx_out):
    def project(h):
        b, s, _ = h.shape
        nq = ATTN_HEADS * ATTN_HEAD_DIM
        nk = ATTN_KV_HEADS * ATTN_HEAD_DIM
        q, k, v = jnp.split(h @ w_qkv, [nq, nq + nk], axis=-1)
        q = _rmsnorm_2(q.reshape(b, s, ATTN_HEADS, ATTN_HEAD_DIM), q_gain)
        k = _rmsnorm_2(k.reshape(b, s, ATTN_KV_HEADS, ATTN_HEAD_DIM), k_gain)
        return q, k, v.reshape(b, s, ATTN_KV_HEADS, ATTN_HEAD_DIM)

    b, s = h_lat.shape[:2]
    qc, kc, vc = project(h_ctx)
    ql, kl, vl = project(h_lat)
    ang_r, ang_c = _axial_angles(s)
    ql = _apply_axial_rope(ql, ang_r, ang_c)
    kl = _apply_axial_rope(kl, ang_r, ang_c)
    keys = jnp.concatenate([kl, kc], axis=1)
    vals = jnp.concatenate([vl, vc], axis=1)
    q_blocks = ql.reshape(b, s // Q_BLOCK, Q_BLOCK, ATTN_KV_HEADS, ATTN_GROUP, ATTN_HEAD_DIM)
    q_blocks = q_blocks.transpose(1, 0, 2, 3, 4, 5)
    o = lax.map(lambda qb: _gqa(qb, keys, vals), q_blocks)
    o = o.transpose(1, 0, 2, 3, 4, 5).reshape(b, s, ATTN_HEADS * ATTN_HEAD_DIM)
    y_lat = o @ w_o
    y_ctx = None
    if need_ctx_out:
        l = h_ctx.shape[1]
        oc = _gqa(qc.reshape(b, l, ATTN_KV_HEADS, ATTN_GROUP, ATTN_HEAD_DIM), kc, vc)
        y_ctx = oc.reshape(b, l, ATTN_HEADS * ATTN_HEAD_DIM) @ w_o
    return y_lat, y_ctx

def _retention_chunks(q, k, v, log_gamma, state):
    b, h, s, _ = q.shape
    dv = v.shape[-1]
    n = s // RET_CHUNK

    def chunks(a):
        return jnp.moveaxis(a.reshape(b, h, n, RET_CHUNK, a.shape[-1]), 2, 0)

    idx = jnp.arange(RET_CHUNK, dtype=jnp.float32)
    diff = idx[:, None] - idx[None, :]
    intra = jnp.where(diff >= 0, jnp.exp(jnp.maximum(diff, 0.0) * log_gamma[:, None, None]), 0.0)
    q_dec = jnp.exp((idx + 1.0) * log_gamma[:, None])[None, :, :, None]
    k_dec = jnp.exp((RET_CHUNK - 1.0 - idx) * log_gamma[:, None])[None, :, :, None]
    chunk_dec = jnp.exp(RET_CHUNK * log_gamma)[None, :, None, None]

    def step(r, qkv):
        qc, kc, vc = qkv
        att = jnp.einsum('bhid,bhjd->bhij', qc, kc) * intra
        o = jnp.einsum('bhij,bhje->bhie', att, vc) + jnp.einsum('bhid,bhde->bhie', qc, r) * q_dec
        r = r * chunk_dec + jnp.einsum('bhjd,bhje->bhde', kc * k_dec, vc)
        return r, o

    r, o = lax.scan(step, state, (chunks(q), chunks(k), chunks(v)))
    return jnp.moveaxis(o, 0, 2).reshape(b, h, s, dv), r

def _final_state(k, v, log_gamma):
    l = k.shape[2]
    w = jnp.exp((l - 1.0 - jnp.arange(l, dtype=jnp.float32)) * log_gamma[:, None])
    return jnp.einsum('bhjd,bhje->bhde', k * w[None, :, :, None], v)

def _retention_mixer(h_lat, h_ctx, w_in, decay_logit, gn_w, w_out, need_ctx_out):
    log_gamma = jax.nn.log_sigmoid(decay_logit.astype(jnp.float32))
    nq = RET_HEADS * RET_DK
    nv = RET_HEADS * RET_DV

    def project(h):
        b, s, _ = h.shape
        q, k, v, g = jnp.split(h @ w_in, [nq, 2 * nq, 2 * nq + nv], axis=-1)

        def heads(a, d):
            return a.reshape(b, s, RET_HEADS, d).transpose(0, 2, 1, 3).astype(jnp.float32)
        return heads(q, RET_DK), heads(k, RET_DK) * (RET_DK ** -0.5), heads(v, RET_DV), g

    def flip(a):
        return jnp.flip(a, axis=2)

    def readout(y, g):
        b, h, s, dv = y.shape
        mu = jnp.mean(y, axis=-1, keepdims=True)
        var = jnp.mean(jnp.square(y - mu), axis=-1, keepdims=True)
        yn = (y - mu) * lax.rsqrt(var + EPS) * gn_w.astype(jnp.float32).reshape(1, h, 1, dv)
        yn = yn.transpose(0, 2, 1, 3).reshape(b, s, h * dv).astype(g.dtype)
        return (jax.nn.silu(g) * yn) @ w_out

    y_ctx = None
    if need_ctx_out:
        qc, kc, vc, gc = project(h_ctx)
        zero = jnp.zeros(qc.shape[:2] + (RET_DK, RET_DV), jnp.float32)
        oc_f, r_f = _retention_chunks(qc, kc, vc, log_gamma[0], zero)
        oc_b, r_b = _retention_chunks(flip(qc), flip(kc), flip(vc), log_gamma[1], zero)
        y_ctx = readout(oc_f + flip(oc_b), gc)
    else:
        b, l, _ = h_ctx.shape
        kv_c = (h_ctx @ w_in[:, nq:2 * nq + nv])
        kc = kv_c[..., :nq].reshape(b, l, RET_HEADS, RET_DK).transpose(0, 2, 1, 3).astype(jnp.float32) * (RET_DK ** -0.5)
        vc = kv_c[..., nq:].reshape(b, l, RET_HEADS, RET_DV).transpose(0, 2, 1, 3).astype(jnp.float32)
        r_f = _final_state(kc, vc, log_gamma[0])
        r_b = _final_state(flip(kc), flip(vc), log_gamma[1])
    ql, kl, vl, gl = project(h_lat)
    ol_f, _ = _retention_chunks(ql, kl, vl, log_gamma[0], r_f)
    ol_b, _ = _retention_chunks(flip(ql), flip(kl), flip(vl), log_gamma[1], r_b)
    y_lat = readout(ol_f + flip(ol_b), gl)
    return y_lat, y_ctx

def _conv_ffn(h, w_up, conv_w, conv_b, w_down):
    u = h @ w_up
    up = jnp.pad(u, ((0, 0), (1, 1), (0, 0)))
    u = up[:, :-2] * conv_w[0] + up[:, 1:-1] * conv_w[1] + up[:, 2:] * conv_w[2] + conv_b
    a, v = jnp.split(u, 2, axis=-1)
    return (jax.nn.silu(a) * v) @ w_down

def _layer_counts():
    kinds = [i % N_MIXERS for i in range(DEPTH_2)]
    return kinds.count(MIXER_POOL), kinds.count(MIXER_ATTN), kinds.count(MIXER_RET)

def second_inputs(seed: int = 0) -> dict:
    key = jax.random.key(seed)
    ks = jax.random.split(key, 22)
    n_pool, n_attn, n_ret = _layer_counts()
    d = D_MODEL

    def nrm(k, shape):
        return jax.random.normal(k, shape, jnp.float32)

    def w(k, shape, fan_in, gain=1.0):
        return nrm(k, shape) * (gain * fan_in ** -0.5)

    def ones_noise(k, shape):
        return 1.0 + 0.05 * nrm(k, shape)

    decay_base = jnp.asarray(np.log(2.0 ** (5 + np.arange(RET_HEADS)) - 1.0).astype(np.float32))
    return {
        'x': nrm(ks[0], (BATCH, SEQ, d)),
        'c': nrm(ks[1], (BATCH, d)),
        'ctx': nrm(ks[2], (BATCH, CTX_LEN, d)),
        'c_ctx': nrm(ks[3], (d,)),
        'ada_w': w(ks[4], (DEPTH_2, d, 6 * d), d, 0.5),
        'ada_b': 0.01 * nrm(ks[5], (DEPTH_2, 6 * d)),
        'norm_w': ones_noise(ks[6], (DEPTH_2, 2, d)),
        'pool_w': w(ks[7], (n_pool, 4, POOL_GROUP, POOL_GROUP), POOL_GROUP),
        'pool_b': 0.01 * nrm(ks[8], (n_pool, d)),
        'pool_scale': ones_noise(ks[9], (n_pool, d)),
        'attn_w_qkv': w(ks[10], (n_attn, d, (ATTN_HEADS + 2 * ATTN_KV_HEADS) * ATTN_HEAD_DIM), d),
        'attn_q_gain': ones_noise(ks[11], (n_attn, ATTN_HEAD_DIM)),
        'attn_k_gain': ones_noise(ks[12], (n_attn, ATTN_HEAD_DIM)),
        'attn_w_o': w(ks[13], (n_attn, ATTN_HEADS * ATTN_HEAD_DIM, d), ATTN_HEADS * ATTN_HEAD_DIM),
        'ret_w_in': w(ks[14], (n_ret, d, 2 * RET_HEADS * RET_DK + 2 * RET_HEADS * RET_DV), d),
        'ret_decay_logit': decay_base[None, None, :] + 0.1 * nrm(ks[15], (n_ret, 2, RET_HEADS)),
        'ret_gn_w': ones_noise(ks[16], (n_ret, RET_HEADS * RET_DV)),
        'ret_w_out': w(ks[17], (n_ret, RET_HEADS * RET_DV, d), RET_HEADS * RET_DV),
        'ffn_w_up': w(ks[18], (DEPTH_2, d, 2 * D_FF), d),
        'ffn_conv_w': w(ks[19], (DEPTH_2, CONV_WIDTH, 2 * D_FF), CONV_WIDTH),
        'ffn_conv_b': 0.01 * nrm(ks[20], (DEPTH_2, 2 * D_FF)),
        'ffn_w_down': w(ks[21], (DEPTH_2, D_FF, d), D_FF),
    }

def second_block(x, c, ctx, c_ctx, ada_w, ada_b, norm_w, pool_w, pool_b, pool_scale,
              attn_w_qkv, attn_q_gain, attn_k_gain, attn_w_o,
              ret_w_in, ret_decay_logit, ret_gn_w, ret_w_out,
              ffn_w_up, ffn_conv_w, ffn_conv_b, ffn_w_down):
    ctx_s = ctx
    silu_c = jax.nn.silu(c)
    silu_cc = jax.nn.silu(c_ctx)
    for i in range(DEPTH_2):
        kind = i % N_MIXERS
        j = i // N_MIXERS
        need_ctx_out = any(k % N_MIXERS != MIXER_POOL for k in range(i + 1, DEPTH_2))
        need_ctx_in = need_ctx_out or kind != MIXER_POOL

        sh1, sc1, g1, sh2, sc2, g2 = [m[:, None, :] for m in jnp.split(silu_c @ ada_w[i] + ada_b[i], 6, axis=-1)]
        h = _modulate(_rmsnorm_2(x, norm_w[i, 0]), sh1, sc1)
        hc = None
        if need_ctx_in:
            csh1, csc1, cg1, csh2, csc2, cg2 = jnp.split(silu_cc @ ada_w[i] + ada_b[i], 6, axis=-1)
            hc = _modulate(_rmsnorm_2(ctx_s, norm_w[i, 0]), csh1, csc1)

        if kind == MIXER_POOL:
            y = _pool_mixer(h, pool_w[j], pool_b[j], pool_scale[j])
            y_c = _pool_mixer(hc, pool_w[j], pool_b[j], pool_scale[j]) if need_ctx_out else None
        elif kind == MIXER_ATTN:
            y, y_c = _attention_mixer(h, hc, attn_w_qkv[j], attn_q_gain[j], attn_k_gain[j], attn_w_o[j], need_ctx_out)
        else:
            y, y_c = _retention_mixer(h, hc, ret_w_in[j], ret_decay_logit[j], ret_gn_w[j], ret_w_out[j], need_ctx_out)

        x = x + g1 * y
        x = x + g2 * _conv_ffn(_modulate(_rmsnorm_2(x, norm_w[i, 1]), sh2, sc2),
                               ffn_w_up[i], ffn_conv_w[i], ffn_conv_b[i], ffn_w_down[i])
        if need_ctx_out:
            ctx_s = ctx_s + cg1 * y_c
            ctx_s = ctx_s + cg2 * _conv_ffn(_modulate(_rmsnorm_2(ctx_s, norm_w[i, 1]), csh2, csc2),
                                            ffn_w_up[i], ffn_conv_w[i], ffn_conv_b[i], ffn_w_down[i])
    return x


def setup_inputs(seed=0):
    out = dict(first_inputs(seed))
    for name, value in second_inputs(seed + 1).items():
        if name != "x":
            out[name + "_2"] = value
    return out


def reference(
    x, norm1_g, w_in, conv_w, gdn_a_log, gdn_dt_bias, gdn_norm_g, mlstm_i_bias, mlstm_f_bias,
    mlstm_norm_g, w_out, norm2_g, peer_wq, peer_keys, peer_u, peer_v, normf_g, c_2, ctx_2,
    c_ctx_2, ada_w_2, ada_b_2, norm_w_2, pool_w_2, pool_b_2, pool_scale_2, attn_w_qkv_2,
    attn_q_gain_2, attn_k_gain_2, attn_w_o_2, ret_w_in_2, ret_decay_logit_2, ret_gn_w_2,
    ret_w_out_2, ffn_w_up_2, ffn_conv_w_2, ffn_conv_b_2, ffn_w_down_2,
):
    x = first_block(
        x, norm1_g, w_in, conv_w, gdn_a_log, gdn_dt_bias, gdn_norm_g, mlstm_i_bias,
        mlstm_f_bias, mlstm_norm_g, w_out, norm2_g, peer_wq, peer_keys, peer_u, peer_v, normf_g,
    )
    return second_block(
        x, c_2, ctx_2, c_ctx_2, ada_w_2, ada_b_2, norm_w_2, pool_w_2, pool_b_2, pool_scale_2,
        attn_w_qkv_2, attn_q_gain_2, attn_k_gain_2, attn_w_o_2, ret_w_in_2, ret_decay_logit_2,
        ret_gn_w_2, ret_w_out_2, ffn_w_up_2, ffn_conv_w_2, ffn_conv_b_2, ffn_w_down_2,
    )


_drawn_inputs = setup_inputs


def setup_inputs(seed=0):
    import zlib

    import numpy as np

    out = dict(_drawn_inputs(seed))
    spreads = {}
    factors = {'gdn_norm_g': 3.17,
     'mlstm_i_bias': 5.851,
     'mlstm_norm_g': 3.609,
     'normf_g': 2.753,
     'ctx_2': 3.477,
     'ada_b_2': 3.755,
     'pool_b_2': 8.0,
     'pool_scale_2': 3.962,
     'attn_q_gain_2': 8.0,
     'attn_k_gain_2': 8.0,
     'ffn_conv_b_2': 31.143,
     'norm2_g': 3.273}
    for name, (base, spread) in spreads.items():
        noise = np.random.default_rng([zlib.crc32(name.encode()), seed]).standard_normal(out[name].shape)
        drawn = base * np.exp(spread * noise) if base else spread * noise
        out[name] = __import__('jax').numpy.asarray(drawn.astype(out[name].dtype))
    for name, factor in factors.items():
        out[name] = (out[name] * factor).astype(out[name].dtype)
    return out
```

```python
import numpy as np
import concourse.bass as bass
from concourse import mybir
from contextlib import ExitStack


def shape_constants():
    f = np.float32
    i = np.arange(128)
    ident = np.eye(128, dtype=f)
    lo = (i[:, None] <= i[None, :]).astype(f)
    hi = (i[:, None] >= i[None, :]).astype(f)
    one, zero = np.ones((128, 128), f), np.zeros((128, 128), f)
    mask2f = np.concatenate([lo, one, zero, lo], 1)
    mask2b = np.concatenate([hi, zero, one, hi], 1)
    swap = np.zeros((128, 128), f)
    for base in (0, 64):
        for r in range(32):
            swap[base + 32 + r, base + r] = -1.0
            swap[base + r, base + 32 + r] = 1.0
    iota = np.broadcast_to(np.arange(16, dtype=f), (128, 16))
    base = np.concatenate([ident, lo, hi, mask2f, mask2b, swap, iota], 1)
    levels = []
    for d in range(2):
        for l in range(7):
            b = 1 << l
            same = (i[:, None] // (2 * b)) == (i[None, :] // (2 * b))
            first = (i // b) % 2 == 0
            m = same & first[:, None] & ~first[None, :]
            levels.append((m if d == 0 else m.T).astype(f))
    levels = np.concatenate(levels, 1)
    t = np.arange(256)
    inv = np.power(10000.0, -np.arange(0, 64, 2, dtype=np.float32) / 64).astype(f)
    row = (t // 64).astype(f)[:, None] * inv
    col = (t % 64).astype(f)[:, None] * inv
    ang = np.concatenate([row, row, col, col], 1).T
    cnt = []
    for win in (2, 4, 8, 16):
        a = np.clip(t - win // 2, 0, 256)
        b = np.clip(t + win // 2, 0, 256)
        cnt.append((1.0 / (b - a)).astype(f))
    cnt = np.broadcast_to(np.concatenate(cnt), (128, 1024))
    late = np.concatenate([np.cos(ang).astype(f), np.sin(ang).astype(f), cnt], 1)
    return (np.ascontiguousarray(base, f), np.ascontiguousarray(levels, f), np.ascontiguousarray(late, f))


def program(nc, a, out, stop=99, taps=None):
    F32, U32 = mybir.dt.float32, mybir.dt.uint32
    ALU, ACT, AX = mybir.AluOpType, mybir.ActivationFunctionType, mybir.AxisListType
    MUL, ADD, SUB, MAX, MIN = ALU.mult, ALU.add, ALU.subtract, ALU.max, ALU.min
    ctx = ExitStack()
    taps = taps or {}
    PEK, EVERY = 3, 5

    class Queue:
        def __init__(self, name, chained):
            self.sem = ctx.enter_context(nc.semaphore("s_" + name))
            self.count, self.items, self.chained = 0, [], chained

        def __call__(self, fn, *waits, free=False):
            waits = list(flat(waits))
            if self.chained and self.count and not free:
                waits.append((self.sem, self.count))
            self.count += 1
            self.items.append((waits, fn, self.sem, 1))
            return (self.sem, self.count)

        def dma(self, fn, line, *waits):
            line.count += 16
            self.items.append((list(flat(waits)), fn, line.sem, 16))
            return (line.sem, line.count)

        def play(self, eng):
            seen = {}
            for waits, fn, sem, inc in self.items:
                for s, v in waits:
                    if seen.get(id(s), 0) < v:
                        eng.wait_ge(s, v)
                        seen[id(s)] = v
                fn().then_inc(sem, inc)

    class Line:
        def __init__(self, name):
            self.sem, self.count = ctx.enter_context(nc.semaphore("d_" + name)), 0

    def flat(x):
        for t in x:
            if t is None:
                continue
            if isinstance(t, list):
                yield from flat(t)
            else:
                yield t

    PE, V, A, G, SP = Queue("pe", False), Queue("dve", True), Queue("act", True), Queue("pool", True), Queue("sp", False)
    vec, act, pool, pe = nc.vector, nc.scalar, nc.gpsimd, nc.tensor

    def sb(name, n, dt=F32, p=128):
        return ctx.enter_context(nc.sbuf_tensor(name, [p, n], dt))

    def bc(ap, n, at=None):
        v = ap.unsqueeze(len(ap.shape) if at is None else at)
        shape = list(v.shape)
        shape[len(ap.shape) if at is None else at] = n
        return v.broadcast_to(shape)

    cbase = sb("cbase", 128 * 12 + 16)
    ident, lo, hi = cbase[:, 0:128], cbase[:, 128:256], cbase[:, 256:384]
    mask2 = [cbase[:, 384:896], cbase[:, 896:1408]]
    swap, iota16 = cbase[:, 1408:1536], cbase[:, 1536:1552]
    tri = [lo, hi]
    ones = sb("ones", 128)[:, :]
    eps = sb("eps", 1)[:, :]
    cl = sb("cl", 1792)
    cosT, sinT, rcnt = cl[:, 0:256], cl[:, 256:512], cl[:, 512:1536]
    vecT = sb("vecT", 640)
    convw = sb("convw", 60)
    small = sb("small", 64)
    mods = [sb("mods0", 96), sb("mods1", 96)]
    wring = sb("wring", 4 * 4096)
    arena = sb("arena", 29760)

    class Area:
        def __init__(self, at=0):
            self.at = at

        def take(self, n, dt=None):
            v = arena[:, self.at:self.at + n]
            self.at += n
            assert self.at <= 29760, self.at
            return v if dt is None else v.bitcast(dt)

    class Bank:
        def __init__(self, i):
            t = ctx.enter_context(nc.psum_tensor(f"ps{i}", [128, 512], F32))
            self.ap, self._free, self.held = t[:, :], None, False

        @property
        def free(self):
            return self._free

        @free.setter
        def free(self, token):
            self._free, self.held = token, False

    banks = [Bank(i) for i in range(8)]
    turn, shared = [0], [banks[0:7]]
    bank_ada = banks[7]

    def bank():
        for _ in range(8):
            turn[0] += 1
            b = shared[0][turn[0] % len(shared[0])]
            if not b.held:
                b.held = True
                return b
        raise RuntimeError("every bank is held")

    def run(gen):
        while True:
            try:
                next(gen)
            except StopIteration as e:
                return e.value

    def weave(gens, width):
        gens, live = list(gens), []
        while gens or live:
            while gens and len(live) < width:
                live.append(gens.pop(0))
            for g in list(live):
                try:
                    next(g)
                except StopIteration:
                    live.remove(g)
            yield

    class Slot:
        def __init__(self, i):
            self.ap, self.line, self.ready = wring[:, i * 4096:(i + 1) * 4096], Line(f"w{i}"), None
            self._free, self.held = None, False

        @property
        def free(self):
            return self._free

        @free.setter
        def free(self, token):
            self._free, self.held = token, False

    slots = [Slot(i) for i in range(4)]
    wturn = [0]

    def load(*parts):
        s = slots[wturn[0] % 4]
        wturn[0] += 1
        assert not s.held
        s.held = True
        for put, src in parts:
            s.ready = SP.dma(lambda d=put(s.ap), c=src: nc.sync.dma_start(d, c), s.line, s.free)
        return s

    def kcols(w, c0, n):
        return ((lambda ap: ap[:, 0:8 * n].rearrange("p (k c) -> p k c", k=8)),
                w[:, c0:c0 + n].rearrange("(k p) c -> p k c", p=128))

    def mm(o, l, r, start, stop, *waits):
        return PE(lambda: pe.matmul(o, l, r, start=start, stop=stop), *waits)

    def tr(o, i, *waits):
        n = i.shape[0]
        return PE(lambda: pe.transpose(o, i, ident[0:n, 0:n]), *waits)

    def tt(o, x, y, op, *w, eng=None):
        e, n = (G, pool) if eng is G else (V, vec)
        return e(lambda: n.tensor_tensor(o, x, y, op), *w)

    def ts(o, x, s1, s2, op0, op1, *w):
        return V(lambda: vec.tensor_scalar(o, x, s1, s2, op0, op1), *w)

    def stt(o, x, s, y, op0, op1, *w):
        return V(lambda: vec.scalar_tensor_tensor(o, x, s, y, op0, op1), *w)

    def actf(o, x, f, *w, bias=0.0, scale=1.0, accum=None):
        return A(lambda: act.activation(o, x, f, bias=bias, scale=scale, accum_out=accum), *w)

    def copyA(o, x, *w):
        return A(lambda: act.activation(o, x, ACT.Copy), *w)

    def copyV(o, x, *w):
        return V(lambda: vec.tensor_copy(o, x), *w)

    def recip(o, x, *w):
        return V(lambda: vec.reciprocal(o, x), *w)

    tapl = Line("tap")

    def tap(name, ap, *w):
        if name in taps:
            SP.dma(lambda: nc.sync.dma_start(taps[name], ap), tapl, *w)

    l_c, l_x, l_v, l_s = Line("c"), Line("x"), Line("v"), Line("s")

    def ld(o, src, line, *w):
        return SP.dma(lambda: nc.sync.dma_start(o, src), line, *w)

    ar = Area()
    x1 = ar.take(2048).rearrange("p (t d) -> p t d", t=2)
    hT = ar.take(2048).rearrange("p (c n) -> p c n", c=8)
    raw = ar.take(12 * 260).rearrange("p (b n) -> p b n", b=12)
    zT, mqT, mkT, moT = (ar.take(1024).rearrange("p (b n) -> p b n", b=4) for _ in range(4))
    mv = ar.take(1032).rearrange("p (t h e) -> p t h e", t=2, h=4)
    qkv_at = ar.at
    qkv = ar.take(3072).rearrange("p (b n) -> p b n", b=12)
    ktok = ar.take(1024).rearrange("p (t h e) -> p t h e", t=2, h=4)
    vtok = ar.take(1024).rearrange("p (t h e) -> p t h e", t=2, h=4)
    mark = ar.at
    ET, AT, PQ, OT, DD, DT = (ar.take(2048).rearrange("p (m n) -> p m n", m=16) for _ in range(6))
    gt = sb("gt", 340)[:, :]

    xv = a["x"][0].rearrange("(t p) d -> p t d", p=128)
    l_x2 = Line("x2")
    t_x = [ld(x1[:, 0, :], xv[:, 0, :], l_x), ld(x1[:, 1, :], xv[:, 1, :], l_x2)]
    t_c = ld(cbase[:, :], a["c_base"], l_c)
    stage = arena[:, qkv_at:qkv_at + 640].rearrange("p (t c) -> p t c", t=5)
    rows = {}
    at = 0

    def vrow(line, name, src, n):
        nonlocal at
        rows[name] = at
        done = 0
        while done < n:
            t, r = divmod(at, 128)
            m = min(n - done, 128 - r)
            tok = ld(stage[r:r + m, t, :], src[done:done + m, :], line)
            at += m
            done += m
        return tok

    def rr(ap):
        return ap.rearrange("(r c) -> r c", c=128)

    for i, nm in enumerate(["gdn_dt_bias", "gdn_a_log", "mlstm_i_bias", "mlstm_f_bias"]):
        src = a[nm][0].rearrange("a h -> (a h)").partition_broadcast(128)
        t_sm = ld(small[:, 8 * i:8 * i + 8], src, l_s)
    sm = small[:, 0:32]
    vrow(l_v, "n1", rr(a["norm1_g"][0]), 8)
    vrow(l_v, "mln", rr(a["mlstm_norm_g"][0]), 4)
    vrow(l_v, "gdn", rr(a["gdn_norm_g"][0]), 1)
    vrow(l_v, "qg", rr(a["attn_q_gain_2"][0]), 1)
    vrow(l_v, "kg", rr(a["attn_k_gain_2"][0]), 1)
    vrow(l_v, "nf", rr(a["normf_g"]), 8)
    vrow(l_v, "c", rr(a["c_2"][0]), 8)
    vrow(l_v, "cc", rr(a["c_ctx_2"]), 8)
    vrow(l_v, "pb", rr(a["pool_b_2"][0]), 8)
    vrow(l_v, "psc", rr(a["pool_scale_2"][0]), 8)
    vrow(l_v, "nw", a["norm_w_2"].rearrange("a b (r c) -> (a b r) c", c=128), 32)
    t_v = vrow(l_v, "adb0", a["ada_b_2"].rearrange("a (r c) -> (a r) c", c=128)[0:41], 41)

    w_in = a["w_in"][0]
    wg = load(kcols(w_in, 2048, 16))
    wg2ap = wg.ap[:, 128:256].rearrange("p (k c) -> p k c", k=8)
    wg.ready = SP.dma(lambda: nc.sync.dma_start(wg2ap, w_in[:, 4112:4128].rearrange("(k p) c -> p k c", p=128)), wg.line)
    w_k, w_v, w_q = load(kcols(w_in, 512, 512)), load(kcols(w_in, 1024, 512)), load(kcols(w_in, 0, 512))
    t_cw = ld(convw[:, :].rearrange("p (b k) -> p b k", b=12),
              a["conv_w"][0].rearrange("(b p) k -> p b k", p=128), l_s)
    l_v2 = Line("v2")
    vrow(l_v2, "adb1", a["ada_b_2"].rearrange("a (r c) -> (a r) c", c=128)[41:96], 55)
    vrow(l_v2, "cw", a["ffn_conv_w_2"].rearrange("a b (r c) -> (a b r) c", c=128), 264)
    t_v2 = vrow(l_v2, "cb", a["ffn_conv_b_2"].rearrange("a (r c) -> (a r) c", c=128), 88)
    rows["adb"] = rows["adb0"]
    t_cl = ld(cl[:, :], a["c_levels"], l_c)
    t_ones = V(lambda: vec.memset(ones, 1.0))
    t_eps = V(lambda: vec.memset(eps, 1e-6))

    def vcol(name, i=0):
        r = rows[name] + i
        return vecT[:, r:r + 1]

    def vcols(name, n):
        return vecT[:, rows[name]:rows[name] + n]

    def vec_cols(t0, t1, tv):
        for t in range(t0, t1):
            n = min(128, at - 128 * t)
            b = bank()
            tk = tr(b.ap[:, 0:n], stage[0:n, t, :], t_c, tv, b.free)
            k = b.free = copyA(vecT[:, 128 * t:128 * t + n], b.ap[:, 0:n], tk)
        return k, tk

    def token_norm(xt, toks, tmp, ss, out):
        res = []
        for t in range(2):
            s = ss[:, 4 * t:4 * t + 4]
            k = actf(tmp[:, 0:1024], xt[:, t, :], ACT.Square, toks[t], t_eps, accum=s[:, 0:1])
            k = actf(s[:, 1:2], s[:, 0:1], ACT.Sqrt, k, bias=eps, scale=1.0 / 1024)
            k = recip(s[:, 2:3], s[:, 1:2], k)
            res.append(out(t, s[:, 2:3], k))
        return res

    def blocks_T(o, xt, t, c0, tok, evac):
        b = bank()
        for j in range(4):
            k = tr(b.ap[:, 128 * j:128 * j + 128], xt[:, 128 * j:128 * j + 128], tok, b.free)
        b.free = evac(o[:, c0:c0 + 4, 128 * t:128 * t + 128], b.ap.rearrange("p (c n) -> p c n", c=4), c0, k)
        return b.free

    def to_cols(o, xt, toks, evac):
        return [blocks_T(o, xt[:, t, 512 * q:512 * q + 512], t, 4 * q, toks[t], evac) for t in range(2) for q in range(2)]

    xn = arena[:, mark:mark + 2048].rearrange("p (t d) -> p t d", t=2)
    tmp1 = arena[:, mark + 2048:mark + 3072]
    ss = sb("ss", 8)[:, :]
    t_xn = token_norm(x1, t_x, tmp1, ss,
                      lambda t, r, k: ts(xn[:, t, :], x1[:, t, :], r, None, MUL, ALU.bypass, k))
    t_vec, _ = vec_cols(0, 1, t_v)

    def evac_g(name):
        def f(o, p, c0, tok):
            return tt(o, p, bc(vecT[:, rows[name] + c0:rows[name] + c0 + 4], 128), MUL, tok, t_vec)
        return f

    t_hT = to_cols(hT, xn, [[t_xn[0], t_c], [t_xn[1], t_c]], evac_g("n1"))
    tap("hT", hT, t_hT)
    t_pad = V(lambda: vec.memset(raw[:, :, 0:2], 0.0))
    t_pad = V(lambda: vec.memset(raw[:, :, 258:260], 0.0))
    t_one = V(lambda: vec.memset(mv[:, :, :, 128:129], 1.0))

    def mod(l, part, c, s):
        o = ((part * 8) + c) * 2 + s
        return mods[l][:, o:o + 1]

    derived = sb("derived", 2 * 2 * 2 * 8 + 2 * 16 + 16)
    AD = derived[:, 0:64].rearrange("p (l q s c) -> p l q s c", l=2, q=2, s=2)
    PG = derived[:, 64:80].rearrange("p (s c) -> p s c", s=2)
    PB = derived[:, 80:96].rearrange("p (s c) -> p s c", s=2)
    sc16 = derived[:, 96:112].rearrange("p (c s) -> p c s", s=2)
    t_mods = [None, None]

    ahead = []
    ada_at = [0]
    NADA = 24

    def ada_load(n=1):
        for _ in range(n):
            if ada_at[0] < NADA:
                l, g = divmod(ada_at[0], 12)
                ada_at[0] += 1
                ahead.append((l, g, load(kcols(a["ada_w_2"][l], 512 * g, 512))))

    def fill(n=1):
        for _ in range(n):
            if not ahead:
                return
            l, g, s = ahead.pop(0)
            w = s.ap.rearrange("p (k c) -> p k c", k=8)
            for j in range(4):
                o = 96 * l + (4 * g + j) * 2
                for kk in range(8):
                    k = mm(bank_ada.ap[:, o:o + 2], w[:, kk, 128 * j:128 * j + 128], sc16[:, kk, :], kk == 0,
                           kk == 7, s.ready, t_c16, bank_ada.free)
            s.free = ada_done[l] = k

    t_c16 = actf(sc16.rearrange("p c s -> p s c"), vecT[:, rows["c"]:rows["c"] + 16].rearrange("p (s c) -> p s c", s=2),
                 ACT.Silu, t_vec)
    ada_done = [None, None]

    def ada_finish(l):
        mv_ = mods[l][:, 0:96].rearrange("p (b s) -> p b s", s=2)
        k = tt(mv_, bank_ada.ap[:, 96 * l:96 * l + 96].rearrange("p (b s) -> p b s", s=2),
               bc(vecT[:, rows["adb"] + 48 * l:rows["adb"] + 48 * l + 48], 2), ADD, ada_done[l], t_vec, t_vec2)
        if l == 1:
            bank_ada.free = k
        for q in range(2):
            for s_ in range(2):
                part = mods[l][:, 16 * (3 * q + 1):16 * (3 * q + 1) + 16].rearrange("p (c s) -> p c s", s=2)[:, :, s_]
                nw = vecT[:, rows["nw"] + 16 * l + 8 * q:rows["nw"] + 16 * l + 8 * q + 8]
                k = stt(AD[:, l, q, s_, :], part, 1.0, nw, ADD, MUL)
        if l == 0:
            for s_ in range(2):
                g1 = mods[0][:, 32:48].rearrange("p (c s) -> p c s", s=2)[:, :, s_]
                k = tt(PG[:, s_, :], g1, vcols("psc", 8), MUL)
                k = tt(PB[:, s_, :], PG[:, s_, :], vcols("pb", 8), MUL)
        t_mods[l] = k

    def ada_rest(l):
        while ada_at[0] < 12 * (l + 1) or ahead:
            if ada_at[0] < 12 * (l + 1) and len(ahead) < 2:
                ada_load()
            else:
                fill()
            yield
        ada_finish(l)
        yield

    def colproj(s, rhs, toks, consume, nb=4, width=4):
        w = s.ap[:, 0:8 * 128 * width].rearrange("p (k c) -> p k c", k=8)
        for j in range(0, nb, 2):
            b = bank()
            for i in range(2):
                for kk in range(8):
                    k = mm(b.ap[:, 256 * i:256 * i + 256], w[:, kk, 128 * (j + i):128 * (j + i) + 128],
                           rhs[:, kk, :], kk == 0, kk == 7, s.ready, toks, b.free)
            b.free = consume(j, b.ap.rearrange("p (i n) -> p i n", i=2), k)
            s.free = k
        return b.free

    b = bank()
    gv = b.ap[:, 0:64].rearrange("p (t c) -> p t c", t=2)
    wgv = [wg.ap[:, 0:128].rearrange("p (k c) -> p k c", k=8), wg2ap]
    for t in range(2):
        for i in range(2):
            for kk in range(8):
                k = mm(gv[:, t, 16 * i:16 * i + 16], hT[:, kk, 128 * t:128 * t + 128], wgv[i][:, kk, :],
                       kk == 0, kk == 7, wg.ready, t_hT, b.free)
    wg.free = k
    go = [0]

    def gtake(n):
        go[0] += n
        return gt[:, go[0] - n:go[0]]

    GX = gtake(64).rearrange("p (t c) -> p t c", t=2)
    GU = gtake(32).rearrange("p (t c) -> p t c", t=2)
    GE = gtake(32).rearrange("p (t c) -> p t c", t=2)
    GL = gtake(32).rearrange("p (t c) -> p t c", t=2)
    BETA = gtake(16).rearrange("p (t c) -> p t c", t=2)
    na = gtake(8)
    k = tt(GX[:, :, 0:8], gv[:, :, 0:8], bc(sm[:, 0:8], 2, 1), ADD, k, t_sm)
    k = copyV(GX[:, :, 8:16], gv[:, :, 8:16])
    k = tt(GX[:, :, 16:32], gv[:, :, 16:32], bc(sm[:, 16:32], 2, 1), ADD)
    b.free = k
    k = copyV(GU[:, :, 0:8], GX[:, :, 0:8], k)
    k = ts(GU[:, :, 8:16], GX[:, :, 24:32], -1.0, None, MUL, ALU.bypass)
    k2 = actf(BETA, GX[:, :, 8:16], ACT.Sigmoid, k)
    k = stt(GE, GU, -1.0, GU, MUL, MIN)
    k = actf(GE, GE, ACT.Exp, k)
    k = actf(GE, GE, ACT.Ln, k, bias=ones[:, 0:1])
    k3 = actf(na, sm[:, 8:16], ACT.Exp)
    k = stt(GL, GU, 0.0, GE, MAX, ADD, k)
    k = stt(GL[:, :, 0:8], GL[:, :, 0:8], -1.0, bc(na, 2, 1), MUL, MUL, k3)
    t_gl = ts(GL[:, :, 8:16], GL[:, :, 8:16], -1.0, None, MUL, ALU.bypass, k2)
    tap("GL", GL, t_gl)
    tap("BETA", BETA, t_gl)

    def keep(dst, off=0):
        def f(j, p, tok):
            return copyA(dst[:, off + j:off + j + 2, 2:258] if dst is raw else dst[:, off + j:off + j + 2, :], p, tok)
        return f

    t_raw = [colproj(w_k, hT, t_hT, keep(raw, 4))]

    b = bank()
    for d in range(2):
        for t in range(2):
            o = d * 8 + t * 4
            k = mm(b.ap[:, o:o + 4], tri[d], GL[:, t, 4 * d:4 * d + 4], True, True, t_gl, t_c, t_ones, b.free)
            o += 32
            other = (d == 0 and t == 1) or (d == 1 and t == 0)
            k = mm(b.ap[:, o:o + 4], tri[d], GL[:, t, 8 + 4 * d:12 + 4 * d], True, not other)
            if other:
                k = mm(b.ap[:, o:o + 4], ones, GL[:, 1 - t, 8 + 4 * d:12 + 4 * d], False, True)
    for t in range(2):
        k = mm(b.ap[:, 16 + 8 * t:24 + 8 * t], ones, GL[:, t, 0:8], True, True)
    Gc = gtake(16)
    Fc = gtake(16)
    GT = gtake(16)
    CC = gtake(16)
    bt = gtake(16)
    NBE = gtake(16)
    EG = gtake(16)
    EM = gtake(16)
    hdt = lambda ap: ap.rearrange("p (h d t) -> p d t h", h=4, d=2)
    psv = lambda o: b.ap[:, o:o + 16].rearrange("p (d t h) -> p d t h", d=2, t=2)
    k = V(lambda o=hdt(Gc), i=psv(0): vec.tensor_copy(o, i), k)
    k = V(lambda o=Fc.rearrange("p (t d h) -> p d t h", t=2, d=2), i=psv(32): vec.tensor_copy(o, i))
    gtot = b.ap[:, 16:32].rearrange("p (t d h) -> p d t h", t=2, d=2)
    k = tt(hdt(GT), gtot, hdt(Gc), SUB)
    b.free = k
    k = tt(CC.rearrange("p (t c) -> p t c", t=2), GX[:, :, 16:24], Fc.rearrange("p (t c) -> p t c", t=2), SUB)
    k = copyV(hdt(bt), BETA.rearrange("p t (d h) -> p d t h", d=2))
    kE = actf(EG, Gc, ACT.Exp, k)
    kE = actf(GT, GT, ACT.Exp)
    t_cols = stt(NBE, EG, -1.0, bt, MUL, MUL, kE)

    rowt = sb("rowt", 3 * 256, p=8)
    crow, mf, mb = rowt[:, 0:256], rowt[:, 256:512], rowt[:, 512:768]
    b = bank()
    for t in range(2):
        k = tr(b.ap[0:8, 128 * t:128 * t + 128], CC[:, 8 * t:8 * t + 8], t_cols, b.free)
    k = copyV(crow, b.ap[0:8, 0:256], k)
    b.free = k
    k = V(lambda: vec.tensor_tensor_scan(mf, crow, crow, 0.0, MAX, MAX), k)
    k = V(lambda: vec.tensor_tensor_scan(mb[:, ::-1], crow[:, ::-1], crow[:, ::-1], 0.0, MAX, MAX), k)
    k = ts(rowt[:, 256:768], rowt[:, 256:768], -1.0, None, MUL, ALU.bypass)
    t_rows = k
    t_raw.append(colproj(w_v, hT, t_hT, keep(raw, 8)))
    b = bank()
    for d, r in ((0, mf), (1, mb)):
        for t in range(2):
            o = 16 * d + 8 * t
            kk = tr(b.ap[:, o:o + 8], r[:, 128 * t:128 * t + 128], k, b.free)
    for d in range(2):
        k = tt(EM.rearrange("p (h d t) -> p d t h", h=4, d=2)[:, d], b.ap[:, 16 * d:16 * d + 16]
               .rearrange("p (t c) -> p t c", t=2)[:, :, 4 * d:4 * d + 4],
               Fc.rearrange("p (t c) -> p t c", t=2)[:, :, 4 * d:4 * d + 4], SUB, kk)
    b.free = k
    t_em = actf(EM, EM, ACT.Exp, k)

    def conv(g, tk):
        taps0 = []
        for blk in range(4 * g, 4 * g + 4):
            taps0.append(actf(qkv[:, blk, :], raw[:, blk, 0:256], ACT.Copy, tk, t_pad, t_cw, t_stage,
                              scale=convw[:, 5 * blk:5 * blk + 1]))
        for blk in range(4 * g, 4 * g + 4):
            o, k = qkv[:, blk, :], taps0[blk - 4 * g]
            for j in range(1, 5):
                k = stt(o, raw[:, blk, j:j + 256], convw[:, 5 * blk + j:5 * blk + j + 1], o, MUL, ADD, k)
        return actf(qkv[:, 4 * g:4 * g + 4, :], qkv[:, 4 * g:4 * g + 4, :], ACT.Silu, k)

    t_vec2, t_stage = vec_cols(1, 5, t_v2)
    hm = lambda buf, h: buf[:, 4 * h:4 * h + 4, :]
    f2 = lambda ap: ap.rearrange("p m n -> p (m n)")
    t_et = []

    def decays(h):
        bg = bank()
        for d in range(2):
            for t in range(2):
                o = 128 * (2 * d + t)
                k = mm(bg.ap[:, o:o + 128], bc(GL[:, t, 4 * d + h], 128), tri[d], True, True, t_gl, bg.free)
        br = bank()
        for d in range(2):
            for t in range(2):
                o = 128 * (2 * d + t)
                k2 = mm(br.ap[:, o:o + 128], bc(BETA[:, t, 4 * d + h], 128), ident, True, True, t_gl, br.free)
        for m in range(4):
            kx = ts(ET[:, 4 * h + m, :], bg.ap[:, 128 * m:128 * m + 128], Gc[:, 4 * h + m:4 * h + m + 1], 0.0,
                    SUB, MIN, k, t_cols, t_hT)
        bg.free = kx
        kx = actf(f2(hm(ET, h)), f2(hm(ET, h)), ACT.Exp, kx)
        kb = br.free = tt(f2(hm(AT, h)), f2(hm(ET, h)), br.ap, MUL, kx, k2, t_hT)
        t_et.append([kx, kb])

    t_raw.append(colproj(w_q, hT, t_hT, keep(raw, 0)))
    decays(0)
    decays(1)
    cvt, t_l2 = {}, {}
    cvt[1] = conv(1, t_raw[0])
    s = load(kcols(w_in, 3088, 512))
    w = s.ap.rearrange("p (k c) -> p k c", k=8)
    for t in range(2):
        b = bank()
        for kk in range(8):
            k = mm(b.ap, hT[:, kk, 128 * t:128 * t + 128], w[:, kk, :], kk == 0, kk == 7, s.ready, t_hT, b.free)
        t_mv = b.free = copyA(mv[:, t, :, 0:128], b.ap.rearrange("p (h e) -> p h e", h=4), k)
    s.free = k
    decays(2)
    decays(3)
    sqt = f2(OT).rearrange("p (b n) -> p b n", b=8)
    rq = f2(DD).rearrange("p (b n) -> p b n", b=8)

    def l2(g):
        kq = actf(sqt[:, 4 * g:4 * g + 4, :], qkv[:, 4 * g:4 * g + 4, :], ACT.Square, cvt[g])
        parts = []
        for i in range(2):
            c = 4 * g + 2 * i
            b = bank()
            k = mm(b.ap, ones, sqt[:, c:c + 2, :], True, True, kq, b.free)
            parts.append((c, b, k))
        for c, b, k in parts:
            k = b.free = actf(rq[:, c:c + 2, :], b.ap.rearrange("p (i n) -> p i n", i=2), ACT.Sqrt, k, bias=eps)
            k = recip(rq[:, c:c + 2, :], rq[:, c:c + 2, :], k)
            k = stt(qkv[:, c:c + 2, :], qkv[:, c:c + 2, :], (128 ** -0.5, 1.0)[g], rq[:, c:c + 2, :], MUL, MUL)
        return k

    t_q = colproj(load(kcols(w_in, 2064, 512)), hT, t_hT, keep(mqT))
    cvt[2] = conv(2, t_raw[1])
    t_l2[1] = l2(1)
    t_k = colproj(load(kcols(w_in, 2576, 512)), hT, t_hT, keep(mkT))
    cvt[0] = conv(0, t_raw[2])

    QT, KT = qkv[:, 0:4, :], qkv[:, 4:8, :]
    t_at, t_pq = [None] * 4, [None] * 4
    four = lambda ap: ap.rearrange("p (d t) n -> p d (t n)", d=2)

    def tokens_of(src, dst, tok):
        for t in range(2):
            b = bank()
            for h in range(4):
                k = tr(b.ap[:, 128 * h:128 * h + 128], qkv[:, src + h, 128 * t:128 * t + 128], tok, b.free)
            k = b.free = copyA(dst[:, t], b.ap.rearrange("p (h e) -> p h e", h=4), k)
        return k

    for h in range(4):
        bk = bank()
        for t in range(2):
            sl = slice(128 * t, 128 * t + 128)
            k = mm(bk.ap[:, 128 * t:128 * t + 128], KT[:, h, sl], KT[:, h, sl], True, True, t_l2[1], bk.free)
        t_at[h] = bk.free = tt(four(hm(AT, h)), four(hm(AT, h)), bc(bk.ap[:, 0:256], 2, 1), MUL, k, t_et[h])
    t_l2[0] = l2(0)
    t_z = colproj(load(kcols(w_in, 1536, 512)), hT, t_hT,
                  lambda j, p, tok: actf(zT[:, j:j + 2, :], p, ACT.Silu, tok))

    def level(l, dst, free):
        out = []
        for h in range(4):
            for d in range(2):
                msk = cl[:, 128 * (7 * d + l):128 * (7 * d + l) + 128]
                m = 4 * h + 2 * d
                k = tt(dst[:, m:m + 2, :], AT[:, m:m + 2, :], bc(msk, 2, 1), MUL, t_at[h], t_cl, free[h], eng=G)
            out.append(k)
        return out

    raw2 = arena[:, 4096:6144].rearrange("p (m n) -> p m n", m=16)
    OTs = [OT, raw2]
    X = ET
    sq_done = [t_l2[0], (PE.sem, PE.count)]
    k0 = level(0, OT, [t_l2[0]] * 4)
    t_ktok = tokens_of(4, ktok, t_l2[1])
    t_vtok = tokens_of(8, vtok, cvt[2])
    tap("ktok", ktok, t_ktok)
    t_tok = [t_ktok, t_vtok]
    kdt = []
    for h in range(4):
        bk = bank()
        for t in range(2):
            sl = slice(128 * t, 128 * t + 128)
            k = mm(bk.ap[:, 128 * t:128 * t + 128], KT[:, h, sl], QT[:, h, sl], True, True, t_l2[0], t_l2[1], bk.free)
        kk2 = bk.free = tt(four(hm(PQ, h)), four(hm(ET, h)), bc(bk.ap[:, 0:256], 2, 1), MUL, k, t_et[h])
        kdt.append(kk2)
    t_o = colproj(load(kcols(w_in, 3600, 512)), hT, t_hT,
                  lambda j, p, tok: actf(moT[:, j:j + 2, :], p, ACT.Sigmoid, tok))
    pe_proj = (PE.sem, PE.count)
    loaded = [load(kcols(a["w_out"][0], 0, 512)), load(kcols(a["w_out"][0], 512, 512)),
              load((lambda ap: ap[:, 0:2048].rearrange("p (g d) -> p g d", g=16),
                    a["peer_keys"][0].rearrange("h q k d -> k (h q) d"))),
              load(kcols(a["peer_wq"][0], 0, 512))]
    for h in range(4):
        kd0 = tt(hm(DT, h), bc(ident, 4, 1), hm(OT, h), SUB, k0[h])
        kdt[h] = [kd0, kdt[h]]
    lev_ok = {}
    lev_free = [[kdt[h] for h in range(4)], [[t_raw, cvt[0], cvt[1], cvt[2], (V.sem, V.count)]] * 4]
    lev_ok[1] = level(1, OTs[1], lev_free[1])

    kd = []
    for h in range(4):
        b = bank()
        for i in range(4):
            kk = tr(b.ap[:, 128 * i:128 * i + 128], DT[:, 4 * h + i, :], kdt[h], b.free)
        b.free = copyA(hm(DD, h), b.ap.rearrange("p (m n) -> p m n", m=4), kk)
        kd.append([b.free, kdt[h]])

    def head_level(l, h):
        O = OTs[l % 2]
        b = bank()
        for i in range(4):
            m = 4 * h + i
            k = mm(b.ap[:, 128 * i:128 * i + 128], O[:, m, :], DD[:, m, :], True, True, lev_ok[l][h], kd[h], b.free)
        kO = k
        kx = b.free = copyA(f2(hm(X, h)), b.ap, k, kdt[h])
        yield
        b = bank()
        for i in range(4):
            m = 4 * h + i
            k = mm(b.ap[:, 128 * i:128 * i + 128], X[:, m, :], DT[:, m, :], True, True, kx, b.free)
        if l < 6:
            b2 = bank()
            for i in range(4):
                m = 4 * h + i
                k2 = mm(b2.ap[:, 128 * i:128 * i + 128], DT[:, m, :], X[:, m, :], True, True, b2.free)
            kd2 = b2.free = tt(f2(hm(DD, h)), f2(hm(DD, h)), b2.ap, SUB, k2)
        else:
            kd2 = k
        kd1 = b.free = tt(f2(hm(DT, h)), f2(hm(DT, h)), b.ap, SUB, k, kd2)
        kd[h] = [kd1, kd2]
        head_level.o[l % 2][h] = kO
        yield

    head_level.o = [[None] * 4, [None] * 4]

    SC = 128 ** -0.5
    PTs = [arena[:, 2048 + 512 * i:2560 + 512 * i] for i in range(4)]
    Ym = arena[:, 6144:7168].rearrange("p (t c) -> p t c", t=2)
    ptfree = [pe_proj] * 4
    dns = gtake(16)
    ym_tok = [None] * 8

    def mlstm_head(h):
        bs = bank()
        for J in range(2):
            k_s = mm(bs.ap[:, 256 * J:256 * J + 256], mkT[:, h, 128 * J:128 * J + 128], mqT[:, h, :], True, True,
                     t_q, t_k, bs.free)
        brs = []
        for d in range(2):
            br = bank()
            brs.append((br, mm(br.ap[:, 0:256], bc(ident[0:8, 4 * d + h], 128), (mf, mb)[d], True, True, t_rows, t_em, br.free)))
        yield
        for d in range(2):
            r = 4 * d + h
            n = 2 * h + d
            P_ = PTs[n % 4]
            dn = dns[:, 4 * (n % 4):4 * (n % 4) + 4]
            br, kr = brs[d]
            for J in range(2):
                kp = ts(P_[:, 256 * J:256 * J + 256], br.ap[:, 0:256], CC[:, 8 * J + r:8 * J + r + 1], 0.0, ADD, MIN,
                        kr, ptfree[n % 4])
            br.free = kp
            kp = actf(P_, P_, ACT.Exp, kp)
            yield
            kp = stt(P_, P_, SC, bs.ap, MUL, MUL, kp, k_s)
            if d == 1:
                bs.free = kp
            kp = tt(P_, P_, mask2[d], MUL, kp)
            bo = bank()
            for t in range(2):
                js = {(0, 0): [0], (0, 1): [0, 1], (1, 0): [0, 1], (1, 1): [1]}[(d, t)]
                for J in js:
                    k = mm(bo.ap[:, 129 * t:129 * t + 129], P_[:, 256 * J + 128 * t:256 * J + 128 * t + 128],
                           mv[:, J, h, :], J == js[0], J == js[-1], kp, t_mv, t_one, bo.free)
            ptfree[n % 4] = k
            yield
            ob = bo.ap[:, 0:258].rearrange("p (t e) -> p t e", t=2)
            k = stt(dn[:, 0:2], ob[:, :, 128], -1.0, EM[:, 4 * h + 2 * d:4 * h + 2 * d + 2], MUL, MAX, k, t_em)
            k = tt(dn[:, 0:2], dn[:, 0:2], ob[:, :, 128], MAX)
            k = recip(dn[:, 2:4], dn[:, 0:2])
            for t in range(2):
                yo = Ym[:, t, 128 * h:128 * h + 128]
                if d == 0:
                    k = ts(yo, ob[:, t, 0:128], dn[:, 2 + t:3 + t], None, MUL, ALU.bypass, t_raw)
                else:
                    k = stt(yo, ob[:, t, 0:128], dn[:, 2 + t:3 + t], yo, MUL, ADD)
            bo.free = k
            ym_tok[n] = k
        yield

    def mlstm():
        for h in range(4):
            yield from mlstm_head(h)

    ml = mlstm()
    for l in range(1, 7):
        if l == 1:
            for h in range(4):
                for d in range(2):
                    t_pq[h] = tt(PQ[:, 4 * h + 2 * d:4 * h + 2 * d + 2, :], PQ[:, 4 * h + 2 * d:4 * h + 2 * d + 2, :],
                                 bc(tri[d], 2, 1), MUL, kdt[h], eng=G)
        if l > 1:
            lev_ok[l] = level(l, OTs[l % 2], lev_free[l % 2])
        hs = [head_level(l, h) for h in range(4)]
        for part in range(2):
            for h in range(4):
                next(hs[h], None)
                if (2 * h + part) % 3 != 0:
                    next(ml, None)
        lev_free[l % 2] = list(head_level.o[l % 2])
    run(ml)
    t_T = kd
    tap("DT", DT, t_T)
    pe_T = (PE.sem, PE.count)

    BV = AT
    kb = [None] * 4
    for h in range(4):
        for d in range(2):
            kb[h] = tt(BV[:, 4 * h + 2 * d:4 * h + 2 * d + 2, :], vtok[:, :, h, :],
                       bc(bt[:, 4 * h + 2 * d:4 * h + 2 * d + 2], 128), MUL, lev_ok[6], t_tok, eng=G)
    KD = X
    kkd = None
    for h in range(4):
        for d in range(2):
            m = 4 * h + 2 * d + d
            kkd = ts(KD[:, 2 * h + d, :], ktok[:, d, h, :], GT[:, m:m + 1], None, MUL, ALU.bypass, t_T, pe_T)
    VN = DD
    S1 = X[:, 8:16, :]
    vn_of = lambda d, t: VN.rearrange("p (h e) n -> p e h n", h=4)[:, 2 * d + t]
    quad = lambda b: b.ap.rearrange("p (h n) -> p h n", h=4)
    kv, ks, QS = {}, [None] * 2, [None] * 2

    def state(d):
        b = bank()
        for h in range(4):
            m = 4 * h + 2 * d + d
            k = mm(b.ap[:, 128 * h:128 * h + 128], DT[:, m, :], BV[:, m, :], True, True, t_T, kb, kkd, b.free)
        kv[d, d] = b.free = copyA(vn_of(d, d), quad(b), k, pe_T)
        yield
        b = bank()
        for h in range(4):
            m = 4 * h + 2 * d + d
            k = mm(b.ap[:, 128 * h:128 * h + 128], KD[:, 2 * h + d, :], VN[:, m, :], True, True, kv[d, d], b.free)
        ks[d] = b.free = copyA(S1.rearrange("p (h e) n -> p e h n", h=4)[:, d], quad(b), k)
        yield
        u = 1 - d
        b = bank()
        for h in range(4):
            k = mm(b.ap[:, 128 * h:128 * h + 128], KT[:, h, 128 * u:128 * u + 128], S1[:, 2 * h + d, :], True, True,
                   ks[d], b.free)
        for h in range(4):
            m = 4 * h + 2 * d + u
            kr = stt(BV[:, m, :], b.ap[:, 128 * h:128 * h + 128], NBE[:, m:m + 1], BV[:, m, :], MUL, ADD, k)
        b.free = kr
        yield
        b = bank()
        for h in range(4):
            k = mm(b.ap[:, 128 * h:128 * h + 128], QT[:, h, 128 * u:128 * u + 128], S1[:, 2 * h + d, :], True, True, b.free)
        QS[d] = (b, k)
        b2 = bank()
        for h in range(4):
            m = 4 * h + 2 * d + u
            k = mm(b2.ap[:, 128 * h:128 * h + 128], DT[:, m, :], BV[:, m, :], True, True, kr, b2.free)
        kv[d, u] = b2.free = copyA(vn_of(d, u), quad(b2), k)
        yield

    for _ in weave([state(0), state(1)], 2):
        pass
    Yg = arena[:, mark + 6144:mark + 7168].rearrange("p (t c) -> p t c", t=2)
    yT = arena[:, mark:mark + 2048].rearrange("p (c n) -> p c n", c=8)
    ysq = arena[:, mark + 7168:mark + 8192]
    yrs = gt[:, 0:16]

    def evac_y(o, p, c0, tok, t):
        sl = slice(128 * t, 128 * t + 128)
        if c0 == 0:
            return stt(o, p, vcol("gdn"), zT[:, :, sl], MUL, MUL, tok, t_z, t_vec)
        k = tt(o, p, moT[:, :, sl], MUL, tok, t_o)
        return tt(o, o, bc(vcols("mln", 4), 128), MUL)

    def head_norm_T(Y, t, c0, tok, free):
        sq = ysq[:, 0:512] if c0 == 0 else ysq[:, 512:1024]
        rs = yrs[:, (c0 + 4 * t):(c0 + 4 * t) + 4] if c0 == 0 else yrs[:, 8 + 4 * t:12 + 4 * t]
        y = Y[:, t, :]
        k = tt(sq, y, y, MUL, tok, pe_T)
        k = V(lambda: vec.tensor_reduce(rs, sq.rearrange("p (h e) -> p h e", h=4), AX.X, ADD))
        k = actf(rs, rs, ACT.Sqrt, k, bias=eps, scale=1.0 / 128)
        yield
        k = recip(rs, rs, k)
        yv = y.rearrange("p (h e) -> p h e", h=4)
        k = tt(yv, yv, bc(rs, 128), MUL)
        yield
        head_norm_T.done.append(blocks_T(yT, y, t, c0, [k, free], lambda o, p, c, tk: evac_y(o, p, c, tk, t)))

    head_norm_T.done = []
    x_free = [(PE.sem, PE.count)]

    def gdn_out(t):
        b = bank()
        for h in range(4):
            for d in range(2):
                m = 4 * h + 2 * d + t
                k = mm(b.ap[:, 128 * h:128 * h + 128], PQ[:, m, :], VN[:, m, :], d == 0, d == 1, kv[d, t], t_pq, b.free)
        kc = b.free = copyA(Yg[:, t, :], b.ap, k, pe_T)
        d = 1 - t
        bq, kq = QS[d]
        yield
        for h in range(4):
            m = 4 * h + 2 * d + t
            ky = stt(Yg[:, t, 128 * h:128 * h + 128], bq.ap[:, 128 * h:128 * h + 128], EG[:, m:m + 1],
                     Yg[:, t, 128 * h:128 * h + 128], MUL, ADD, kc, kq)
        bq.free = ky
        yield from head_norm_T(Yg, t, 0, ky, x_free)

    for _ in weave([gdn_out(0), gdn_out(1), head_norm_T(Ym, 0, 4, ym_tok, x_free), head_norm_T(Ym, 1, 4, ym_tok, x_free)], 4):
        pass
    t_yT = head_norm_T.done
    tap("yT", yT, t_yT)
    lev_last = list(lev_ok[6])
    g2b = cl[:, 0:1024]
    l_g2 = Line("g2")
    t_g2 = ld(g2b, a["norm2_g"][0].partition_broadcast(128), l_g2, lev_last)
    t_x1 = [[], []]
    for half in range(2):
        s = loaded[half]
        w = s.ap.rearrange("p (k c) -> p k c", k=8)
        for t in range(2):
            b = bank()
            for kk in range(8):
                k = mm(b.ap, yT[:, kk, 128 * t:128 * t + 128], w[:, kk, :], kk == 0, kk == 7, s.ready, t_yT, b.free)
            xo = x1[:, t, 512 * half:512 * half + 512]
            b.free = tt(xo, xo, b.ap, ADD, k)
            t_x1[t].append(b.free)
        s.free = k
        loaded.append(load(kcols(a["peer_wq"][0], 512 * (half + 1), 512)))
    tap("x1", x1, t_x1)

    NR = 5
    ar = Area(2048)
    h2 = ar.take(2048).rearrange("p (t d) -> p t d", t=2)
    sco = ar.take(4096).rearrange("p (t g n) -> p t g n", t=2, g=16)
    ring = ar.take(2 * NR * 1024).rearrange("p (s d) -> p s d", s=2 * NR)
    own = ar.at
    xcT = ar.take(2048).rearrange("p (c n) -> p c n", c=8)
    hcT = ar.take(2048).rearrange("p (c n) -> p c n", c=8)
    actT = ar.take(22 * 256).rearrange("p (b n) -> p b n", b=22)
    pt = ar.take(1250)
    end1 = [(PE.sem, PE.count), (V.sem, V.count), (A.sem, A.count), (G.sem, G.count)]
    h2T = arena[:, own:own + 2048].rearrange("p (c n) -> p c n", c=8)
    qryT = [arena[:, own + 2048 + 1024 * i:own + 3072 + 1024 * i].rearrange("p (g n) -> p g n", g=4) for i in range(2)]
    keyT = arena[:, own + 4096:own + 6144].rearrange("p (g n) -> p g n", g=16)
    tmpA = arena[:, own + 6144:own + 7168]
    s = loaded[2]
    kv_ = s.ap[:, 0:2048].rearrange("p (g d) -> p g d", g=16)
    for g in range(0, 16, 4):
        b = bank()
        for i in range(4):
            k = tr(b.ap[:, 128 * i:128 * i + 128], kv_[:, g + i, :], s.ready, b.free)
        t_key = b.free = copyA(keyT[:, g:g + 4, :], b.ap.rearrange("p (i n) -> p i n", i=4), k, end1)
    s.free = k
    t_h2 = token_norm(x1, [[t_x1[0], end1], [t_x1[1], end1]], tmpA, ss,
                      lambda t, r, k: stt(h2[:, t, :], x1[:, t, :], r, g2b, MUL, MUL, k, t_g2, end1))
    t_h2T = to_cols(h2T, h2, t_h2, lambda o, p, c0, tok: copyA(o, p, tok, end1))
    t_sco = []
    qfree = [None, None]
    for q in range(4):
        s = loaded[3 + q] if q < 3 else load(kcols(a["peer_wq"][0], 512 * q, 512))
        Q = qryT[q % 2]
        k = colproj(s, h2T, t_h2T, lambda j, p, tok, Q=Q, q=q: copyA(Q[:, j:j + 2, :], p, tok, qfree[q % 2]))
        both = []
        for t in range(2):
            b = bank()
            for i in range(4):
                g = 4 * q + i
                kk = mm(b.ap[:, 128 * i:128 * i + 128], Q[:, i, 128 * t:128 * t + 128], keyT[:, g, :], True, True,
                        k, t_key, b.free)
            b.free = copyA(sco[:, t, 4 * q:4 * q + 4, :], b.ap.rearrange("p (i n) -> p i n", i=4), kk, end1)
            both.append(b.free)
        qfree[q % 2] = kk
        t_sco.append(both)
    tap("h2", h2, t_h2)
    tap("sco", sco, t_sco)
    prep_done = [(PE.sem, PE.count), (A.sem, A.count)]

    po = [0]

    def pk(n, dt=None):
        po[0] += n
        assert po[0] <= 1250
        v = pt[:, po[0] - n:po[0]]
        return v if dt is None else v.bitcast(dt)

    top = pk(32)
    topi = pk(32, U32)
    topf = pk(32)
    cand = pk(256)
    best = pk(16)
    posu = pk(16, U32)
    ij = pk(32, U32)
    ijf = pk(32)
    oh = pk(512)
    selv = pk(32)
    idf = pk(16)
    idx = [pk(16, U32) for _ in range(3)]
    dots = [pk(16), pk(16)]
    nmx = pk(1)
    exs = [pk(16), pk(16)]
    ssm = [pk(2), pk(2)]
    gl = pk(16)
    wt = [pk(16), pk(16)]
    LOW = -3.0e38
    last_use = [None] * 3
    hts = [(t, h) for h in range(8) for t in range(2)]
    gate_read = [None, None]

    def topk(i):
        t, h = hts[i]
        for p in range(2):
            sc = sco[:, t, 2 * h + p, :]
            for r in range(2):
                o = slice(16 * p + 8 * r, 16 * p + 8 * r + 8)
                V(lambda o=top[:, o], s=sc: vec.max(o, s), t_sco[h // 2][t], end1)
                V(lambda o=topi[:, o], m=top[:, o], s=sc: vec.max_index(o, m, s))
                if r == 0:
                    V(lambda m=top[:, o], s=sc: vec.match_replace(s, m, s, LOW))
            yield
        copyV(topf, topi)
        cv = cand.rearrange("p (a b) -> p a b", a=16)
        tt(cv, bc(top[:, 0:16], 16), bc(top[:, 16:32], 16, 1), ADD)
        V(lambda: vec.max(best[:, 0:8], cand), topk.best_read)
        V(lambda: vec.max_index(posu[:, 0:8], best[:, 0:8], cand))
        yield
        V(lambda: vec.match_replace(cand, best[:, 0:8], cand, LOW))
        V(lambda: vec.max(best[:, 8:16], cand))
        k = V(lambda: vec.max_index(posu[:, 8:16], best[:, 8:16], cand))
        kn = ts(nmx, best[:, 0:1], -1.0, None, MUL, ALU.bypass)
        ke = topk.best_read = actf(exs[i % 2], best, ACT.Exp, kn, gate_read[i % 2], bias=nmx, accum=ssm[i % 2][:, 0:1])
        yield
        ts(ij[:, 0:16], posu, 4, None, ALU.logical_shift_right, ALU.bypass)
        ts(ij[:, 16:32], posu, 15, None, ALU.bitwise_and, ALU.bypass)
        copyV(ijf, ij)
        ohv = oh.rearrange("p (q a) -> p q a", q=32)
        tt(ohv, bc(ijf, 16), bc(iota16, 32, 1), ALU.is_equal)
        yield
        tt(ohv.rearrange("p (w q) a -> p w q a", w=2), ohv.rearrange("p (w q) a -> p w q a", w=2),
           bc(topf.rearrange("p (w a) -> p w a", w=2), 16, 2), MUL)
        V(lambda: vec.tensor_reduce(selv, ohv, AX.X, ADD))
        stt(idf, selv[:, 0:16], 128.0, selv[:, 16:32], MUL, ADD)
        topk.done = copyV(idx[i % 3], idf, last_use[i % 3])
        recip(ssm[i % 2][:, 1:2], ssm[i % 2][:, 0:1], ke)
        yield

    topk.best_read = None
    u_tab, v_tab = a["peer_u"][0], a["peer_v"][0]
    lines = [Line(f"gr{i}") for i in range(2 * NR)]
    rfree = [end1] * (2 * NR)
    rcount = [0, 0]
    vb = [banks[5], banks[6]]
    diag = [cl[:, 1536:1664], cl[:, 1664:1792]]
    dfree = [lev_last, lev_last]
    wtok = [None, None]
    on_pe = lambda k: k % PEK != 0
    ndiag = [0]
    state_v = {}

    def gelu_weights(j):
        kg = actf(gl, dots[j % 2], ACT.Gelu, state_v["dots", j], state_v.get("w", None))
        state_v["gelu", j] = kg

    def weights(j):
        state_v["w"] = gate_read[j % 2] = wtok[j % 2] = stt(
            wt[j % 2], exs[j % 2], ssm[j % 2][:, 1:2], gl, MUL, MUL, state_v["gelu", j], state_v.get(("used", j - 2)))

    def add_pe(j):
        t, h = hts[j]
        for i in range(2):
            k = vb[i].free = tt(x1[:, t, 512 * i:512 * i + 512], x1[:, t, 512 * i:512 * i + 512], vb[i].ap, ADD,
                                state_v["pe", j])

    pe_first = min(k for k in range(16) if on_pe(k))
    pe_last = max(k for k in range(16) if on_pe(k))

    def consume(item):
        kind, j, k, r, tok = item
        t, h = hts[j]
        if kind == "u":
            rfree[r] = V(lambda o=ring[:, r, :], x=h2[:, t, :], c=dots[j % 2][:, k:k + 1]:
                         vec.tensor_tensor_reduce(out=o, in0=o, in1=x, scale=1.0, scalar=0.0,
                                                  op0=MUL, op1=ADD, accum_out=c), tok, state_v.get(("gelu", j - 2)),
                         free=True)
            state_v["dots", j] = rfree[r]
            if k == 15:
                gelu_weights(j)
        elif on_pe(k):
            n = ndiag[0] % 2
            ndiag[0] += 1
            kd_ = actf(diag[n], ident, ACT.Copy, wtok[j % 2], dfree[n], scale=wt[j % 2][:, k:k + 1])
            for i in range(2):
                kp = mm(vb[i].ap, diag[n], ring[:, r, 512 * i:512 * i + 512], k == pe_first, k == pe_last, kd_, tok,
                        vb[i].free)
            dfree[n] = rfree[r] = kp
            state_v["used", j] = [kp, kd_, state_v.get("acc")]
            if k == pe_last:
                state_v["pe", j] = kp
        else:
            rfree[r] = state_v["acc"] = stt(x1[:, t, :], ring[:, r, :], wt[j % 2][:, k:k + 1], x1[:, t, :], MUL, ADD, tok, wtok[j % 2])

    def peer():
        for _ in topk(0):
            yield
        pend = []
        for i in range(17):
            tix = topk.done
            nxt = topk(i + 1) if i + 1 < 16 else iter(())
            steps = []
            for k in range(16):
                if i < 16:
                    steps.append(("u", i, k))
                if i > 0:
                    steps.append(("v", i - 1, k))
            wrote = i == 0
            done = 0
            for kind, j, k in steps:
                r = NR * (kind == "v") + rcount[kind == "v"] % NR
                rcount[kind == "v"] += 1
                tab = u_tab if kind == "u" else v_tab
                tok = G.dma(lambda o=ring[:, r, :], x=idx[j % 3][:, k:k + 1], tb=tab: pool.indirect_dma_start(
                    out=o, out_offset=None, in_=tb, in_offset=bass.IndirectOffsetOnAxis(ap=x, axis=0)),
                    lines[r], tix, rfree[r])
                if kind == "v":
                    last_use[j % 3] = tok
                pend.append((kind, j, k, r, tok))
                done += 1
                if len(pend) >= NR:
                    it = pend.pop(0)
                    if it[0] == "v" and it[1] == i - 1 and not wrote:
                        weights(i - 1)
                        wrote = True
                    consume(it)
                if done % 3 == 0:
                    next(nxt, None)
                yield
            while pend:
                it = pend.pop(0)
                if it[0] == "v" and not wrote:
                    weights(i - 1)
                    wrote = True
                consume(it)
                yield
            for _ in nxt:
                pass
            if i > 0:
                add_pe(i - 1)

    rs_used = [None]

    def modulated(hT_, xT, l, q, s, tok, sqb, rsb, pad=0):
        k = actf(sqb, xT, ACT.Square, tok, rs_used[0])
        yield
        b = bank()
        for c in range(8):
            k2 = mm(b.ap[:, 0:256], ones, sqb[:, c, :], c == 0, c == 7, k, b.free)
        k = b.free = actf(rsb, b.ap[:, 0:256], ACT.Sqrt, k2, bias=eps, scale=1.0 / 1024)
        yield
        recip(rsb, rsb, k)
        toks = []
        for c in range(8):
            o = hT_[:, c, pad:pad + 256]
            k = stt(o, xT[:, c, :], AD[:, l, q, s, c:c + 1], rsb, MUL, MUL, t_mods[l])
            toks.append(actf(o, o, ACT.Identity, k, bias=mod(l, 3 * q, c, s)))
        rs_used[0] = k
        yield
        return toks

    def ffn(l, s, xT, hT_, actb, sqb, rsb, cvb, tok, res):
        th = yield from modulated(hT_, xT, l, 1, s, tok, sqb, rsb)
        wu, wd = a["ffn_w_up_2"][l], a["ffn_w_down_2"][l]
        cwc = lambda j, blk: vcol("cw", 132 * l + 44 * j + blk)
        cvf = [None, None]
        wv = lambda ap, i: ap.rearrange("p (k i c) -> p k i c", k=8, i=2)[:, :, i, :]

        def after(blk, b, k):
            cv = cvb[blk % 2]
            for i in range(2):
                kc = actf(cv[:, i, :], b.ap[:, 256 * i:256 * i + 256], ACT.Identity, k, cvf[blk % 2],
                          bias=vcol("cb", 44 * l + blk + 22 * i), scale=cwc(1, blk + 22 * i))
            for i in range(2):
                u = b.ap[:, 256 * i:256 * i + 256]
                kc = stt(cv[:, i, 1:256], u[:, 0:255], cwc(0, blk + 22 * i), cv[:, i, 1:256], MUL, ADD, kc)
                kc = stt(cv[:, i, 0:255], u[:, 1:256], cwc(2, blk + 22 * i), cv[:, i, 0:255], MUL, ADD)
            b.free = kc
            ks_ = actf(cv[:, 0, :], cv[:, 0, :], ACT.Silu, kc)
            cvf[blk % 2] = tt(actb[:, blk, :], cv[:, 0, :], cv[:, 1, :], MUL, ks_, eng=G if res["pool"] else None)
            return cvf[blk % 2]

        late = None
        for g in range(11):
            sl = load((lambda ap: wv(ap, 0), wu[:, 256 * g:256 * g + 256].rearrange("(k p) c -> p k c", p=128)),
                      (lambda ap: wv(ap, 1), wu[:, 2816 + 256 * g:3072 + 256 * g].rearrange("(k p) c -> p k c", p=128)))
            for jb in range(2):
                b = bank()
                for i in range(2):
                    w = wv(sl.ap, i)
                    for kk in range(8):
                        k = mm(b.ap[:, 256 * i:256 * i + 256], w[:, kk, 128 * jb:128 * jb + 128], hT_[:, kk, :],
                               kk == 0, kk == 7, sl.ready, th[kk], b.free)
                sl.free = k
                if late:
                    ka_ = after(*late)
                late = (2 * g + jb, b, k)
                yield
        ka_ = after(*late)
        for half in range(2):
            bs_ = [bank() for _ in range(4)]
            for f0, nf in ((0, 8), (8, 8), (16, 6)):
                sl = load((lambda ap, nf=nf: ap[:, 0:512 * nf].rearrange("p (f c) -> p f c", f=nf),
                           wd[128 * f0:128 * (f0 + nf), 512 * half:512 * half + 512].rearrange("(f p) c -> p f c", p=128)))
                w = sl.ap[:, 0:512 * nf].rearrange("p (f c) -> p f c", f=nf)
                for m in range(4):
                    for f in range(nf):
                        k = mm(bs_[m].ap[:, 0:256], w[:, f, 128 * m:128 * m + 128], actb[:, f0 + f, :],
                               f0 + f == 0, f0 + f == 21, sl.ready, ka_, bs_[m].free)
                    if f0 + nf == 22:
                        c = 4 * half + m
                        bs_[m].free = stt(xT[:, c, :], bs_[m].ap[:, 0:256], mod(l, 5, c, s), xT[:, c, :], MUL, ADD, k)
                        res["tok"] = bs_[m].free
                    yield
                sl.free = k

    def mix_pool(s, xT, hp, s2, s4, rsb, w, tok, wtoks, dmat, rn):
        ta = V(lambda: vec.memset(hp[:, :, 0:8], 0.0), tok)
        ta = V(lambda: vec.memset(hp[:, :, 264:272], 0.0))
        th = yield from modulated(hp, xT, 0, 0, s, tok, dmat, rsb, pad=8)
        toks = []
        for g, win in enumerate((2, 4, 8, 16)):
            c = slice(2 * g, 2 * g + 2)
            H = hp[:, c, :]
            k = tt(s2[:, :, 1:272], H[:, :, 0:271], H[:, :, 1:272], ADD, th)
            cur = s2
            if win >= 4:
                k = tt(s4[:, :, 2:271], s2[:, :, 1:270], s2[:, :, 3:272], ADD)
                cur = s4
            if win >= 8:
                k = tt(s2[:, :, 4:269], s4[:, :, 2:267], s4[:, :, 6:271], ADD)
                cur = s2
            if win >= 16:
                k = tt(s4[:, :, 8:265], s2[:, :, 4:261], s2[:, :, 12:269], ADD)
                cur = s4
            k = tt(dmat[:, c, :], cur[:, :, 8:264], bc(rcnt[:, 256 * g:256 * g + 256], 2, 1), MUL, t_late[0])
            k = tt(dmat[:, c, :], dmat[:, c, :], H[:, :, 8:264], SUB)
            b = bank()
            for j in range(2):
                for kk in range(2):
                    kp = mm(b.ap[:, 256 * j:256 * j + 256], w[:, 2 * g + kk, 128 * j:128 * j + 128], dmat[:, 2 * g + kk, :],
                            kk == 0, kk == 1, wtoks, k, b.free)
            toks.append((b, kp))
            yield
        for g, (b, kp) in enumerate(toks):
            for j in range(2):
                c = 2 * g + j
                kx = stt(xT[:, c, :], b.ap[:, 256 * j:256 * j + 256], PG[:, s, c:c + 1], xT[:, c, :], MUL, ADD, kp)
                kx = ts(xT[:, c, :], xT[:, c, :], PB[:, s, c:c + 1], None, ADD, ALU.bypass)
            b.free = kx
        rn["tok"], rn["pe"] = kx, kp
        yield

    ring_buf = sb("rsb", 256)[:, :]
    cvb = [sb(f"cvb{i}", 512)[:, :].rearrange("p (i n) -> p i n", i=2) for i in range(2)]
    hp = actT.rearrange("p b n -> p (b n)")
    hpc = hp[:, 0:8 * 272].rearrange("p (c n) -> p c n", c=8)
    s2b = hp[:, 2176:2176 + 544].rearrange("p (c n) -> p c n", c=2)
    s4b = hp[:, 2720:2720 + 544].rearrange("p (c n) -> p c n", c=2)
    ctx_res = {"pool": False}
    t_late = [None]

    def pool_w():
        sl = load((lambda ap: ap[:, 0:2048].rearrange("p (g c) -> p g c", g=8),
                   a["pool_w_2"][0].rearrange("g (k p) c -> p (g k) c", p=128)))
        return sl, sl.ap[:, 0:2048].rearrange("p (g c) -> p g c", g=8)

    def context():
        xin = hp[:, 3584:5632].rearrange("p (t d) -> p t d", t=2)
        lc = Line("ctx")
        t = ld(xin, a["ctx_2"][0].rearrange("(t p) d -> p t d", p=128), lc, prep_done, t_h2)
        t_late[0] = ld(cl[:, 0:1536], a["c_late"], l_c, t_h2)
        yield
        tx = to_cols(xcT, xin, [t, t], lambda o, p, c0, tok: copyA(o, p, tok, prep_done))
        yield
        yield from ada_rest(0)
        sl, w = pool_w()
        yield from mix_pool(1, xcT, hpc, s2b, s4b, ring_buf, w, tx, sl.ready, hcT, ctx_res)
        sl.free = ctx_res["pe"]
        tap("xc1", xcT, ctx_res["tok"])
        yield from ffn(0, 1, xcT, hcT, actT, hcT, ring_buf, cvb, [ctx_res["tok"], ctx_res["pe"]], ctx_res)
        tap("xc2", xcT, ctx_res["tok"])
        yield from ada_rest(1)
        thc = yield from modulated(hcT, xcT, 1, 0, 1, [ctx_res["tok"], (PE.sem, PE.count)], hcT, ring_buf)
        skv = load(kcols(a["attn_w_qkv_2"][0], 1024, 512))
        wk = skv.ap.rearrange("p (k c) -> p k c", k=8)
        context.kv = []
        b = bank()
        for hk in range(2):
            for kk in range(8):
                k = mm(b.ap[:, 256 * hk:256 * hk + 256], wk[:, kk, 128 * hk:128 * hk + 128], hcT[:, kk, :], kk == 0,
                       kk == 7, skv.ready, thc, b.free)
        k = b.free = copyA(kc_keep, b.ap, k, ctx_res["tok"])
        context.kv.append(k)
        yield
        for t in range(2):
            b = bank()
            for kk in range(8):
                k = mm(b.ap[:, 0:256], hcT[:, kk, 128 * t:128 * t + 128], wk[:, kk, 256:512], kk == 0, kk == 7, b.free)
            skv.free = k
            b.free = copyA(vc_keep[:, t, :], b.ap[:, 0:256], k)
            context.kv.append(b.free)
            yield

    kvc = xcT.rearrange("p c n -> p (c n)")
    kc_keep = kvc[:, 0:512]
    vc_keep = kvc[:, 512:1024].rearrange("p (t e) -> p t e", t=2)
    shared[0] = banks[0:5] + [banks[7]]
    if stop >= 2:
        g1_, g2_ = peer(), context()
        n, on = 0, True
        while on:
            on = next(g1_, 0) is None
            n += 1
            if n % EVERY == 0:
                next(g2_, None)
        while next(g2_, 1) is None:
            pass
    t_peer = (V.sem, V.count)
    tap("x2", x1, t_peer)
    shared[0] = banks
    endp = [t_peer, (PE.sem, PE.count), (A.sem, A.count), (G.sem, G.count)]
    if stop >= 4:
        ar = Area(2048)
        xT = ar.take(2048).rearrange("p (c n) -> p c n", c=8)
        hlT = ar.take(2048).rearrange("p (c n) -> p c n", c=8)
        sqb = ar.take(2048).rearrange("p (c n) -> p c n", c=8)
        qT = ar.take(2048).rearrange("p (c n) -> p c n", c=8)
        kTt = ar.take(1024).rearrange("p (c n) -> p c n", c=2)
        vt = ar.take(1024).rearrange("p (t e) -> p t e", t=4)
        oT = ar.take(2048).rearrange("p (c n) -> p c n", c=8)
        pr = ar.take(4 * 512)
        prT = ar.take(2 * 1024)
        assert ar.at <= own, ar.at
        rsb = ring_buf
        xn2 = hlT.rearrange("p c n -> p (c n)").rearrange("p (t d) -> p t d", t=2)
        tn = token_norm(x1, [endp, endp], sqb.rearrange("p c n -> p (c n)"), ss,
                        lambda t, r, k: ts(xn2[:, t, :], x1[:, t, :], r, None, MUL, ALU.bypass, k, endp))
        tx = to_cols(xT, xn2, tn, evac_g("nf"))
        tap("xT", xT, tx)
        res = {"pool": True}
        sl, w = pool_w()
        run(mix_pool(0, xT, hpc, s2b, s4b, rsb, w, [tx, endp], sl.ready, sqb, res))
        sl.free = res["pe"]
        tap("xp", xT, res["tok"])
        run(ffn(0, 0, xT, hlT, actT, sqb, rsb, cvb, [res["tok"], res["pe"], tx], res))
        tap("xf0", xT, res["tok"])
        kcc = copyA(kTt[:, :, 256:512], kc_keep.rearrange("p (c n) -> p c n", c=2), context.kv)
        kvv = copyA(vt[:, 2:4, :], vc_keep)
        th = run(modulated(hlT, xT, 1, 0, 0, [res["tok"], (PE.sem, PE.count)], sqb, rsb))
        wqkv = a["attn_w_qkv_2"][0]
        skv = load(kcols(wqkv, 1024, 512))
        wk = skv.ap.rearrange("p (k c) -> p k c", k=8)
        b = bank()
        for hk in range(2):
            for kk in range(8):
                k = mm(b.ap[:, 256 * hk:256 * hk + 256], wk[:, kk, 128 * hk:128 * hk + 128], hlT[:, kk, :], kk == 0,
                       kk == 7, skv.ready, th[kk], b.free)
        kb_ = b.free = copyA(kTt[:, :, 0:256], b.ap.rearrange("p (c n) -> p c n", c=2), k)
        for t in range(2):
            b = bank()
            for kk in range(8):
                k = mm(b.ap[:, 0:256], hlT[:, kk, 128 * t:128 * t + 128], wk[:, kk, 256:512], kk == 0, kk == 7,
                       b.free)
            t_vt = b.free = copyA(vt[:, t, :], b.ap[:, 0:256], k)
        skv.free = k
        t_vt = [t_vt, kvv]
        scr = sqb.rearrange("p c n -> p (c n)")
        scrs = [(scr[:, 0:512], scr[:, 512:1024], scr[:, 1024:1536]),
                (f2(oT)[:, 0:512], f2(oT)[:, 512:1024], f2(oT)[:, 1024:1536]),
                (prT[:, 0:512], prT[:, 512:1024], prT[:, 1024:1536])]
        sfree = [None] * 3
        nh = [0]
        hn = {}

        def headnorm(key, x, gain, tok, rope):
            z = nh[0] % 3
            nh[0] += 1
            sq2, rr_, ro = scrs[z]
            k = actf(sq2, x, ACT.Square, tok, sfree[z])
            yield
            b = bank()
            k = mm(b.ap, ones, sq2, True, True, k, b.free)
            k = b.free = actf(rr_, b.ap, ACT.Sqrt, k, bias=eps, scale=1.0 / 128)
            yield
            k = recip(rr_, rr_, k)
            k = stt(x, x, vcol(gain), rr_, MUL, MUL, tok)
            yield
            b = bank()
            k2 = mm(b.ap[:, 0:256 * rope], swap, x[:, 0:256 * rope], True, True, k, b.free)
            bv = lambda ap: ap.rearrange("p (i n) -> p i n", i=rope)
            xr = x[:, 0:256 * rope]
            k = b.free = tt(bv(ro[:, 0:256 * rope]), bv(b.ap[:, 0:256 * rope]), bc(sinT, rope, 1), MUL, k2)
            yield
            k = tt(bv(xr), bv(xr), bc(cosT, rope, 1), MUL, eng=G, *[k])
            k = tt(xr, xr, ro[:, 0:256 * rope], ADD, k, eng=G)
            hn[key] = sfree[z] = k
            yield

        def pair(i):
            def f(j, p, tok):
                t = copyA(qT[:, 4 * i + j:4 * i + j + 2, :], p, tok)
                pend_h.append(headnorm(("q", 2 * i + j // 2), f2(qT[:, 4 * i + j:4 * i + j + 2, :]), "qg", t, 2))
                return t
            return f

        pend_h = [headnorm(("k", 0), kTt[:, 0, :], "kg", [kb_, kcc], 1), headnorm(("k", 1), kTt[:, 1, :], "kg", [kb_, kcc], 1)]
        for q in range(2):
            colproj(load(kcols(wqkv, 512 * q, 512)), hlT, th, pair(q))
            if q == 0:
                for _ in range(4):
                    for g in pend_h[0:3]:
                        next(g, None)
        for _ in weave(pend_h, 3):
            pass
        tap("qT", qT, list(hn.values()))
        st = sb("st", 4 * 8)
        all_n = list(hn.values())
        prf, ptf2, oT_tok = [None] * 4, [all_n] * 2, [None] * 8

        def head(h):
            PTb = prT[:, 1024 * (h % 2):1024 * (h % 2) + 1024].rearrange("p (j q) -> p j q", j=4)
            bs = []
            for t in range(2):
                b = bank()
                k = mm(b.ap, qT[:, h, 128 * t:128 * t + 128], kTt[:, h // 4, :], True, True, all_n, b.free)
                bs.append((b, k))
            yield
            kp = []
            for t in range(2):
                b, k = bs[t]
                n = (2 * h + t) % 4
                P_ = pr[:, 512 * n:512 * n + 512]
                sx = st[:, 8 * n:8 * n + 8]
                k = V(lambda o=sx[:, 0:1], i=b.ap: vec.tensor_reduce(o, i, AX.X, MAX), k, prf[n])
                k = ts(sx[:, 1:2], sx[:, 0:1], -SC, None, MUL, ALU.bypass)
                k = b.free = actf(P_, b.ap, ACT.Exp, k, prf[n], bias=sx[:, 1:2], scale=SC, accum=sx[:, 2:3])
                kp.append(k)
            yield
            toks = []
            for t in range(2):
                n = (2 * h + t) % 4
                P_ = pr[:, 512 * n:512 * n + 512]
                sx = st[:, 8 * n:8 * n + 8]
                k = recip(sx[:, 3:4], sx[:, 2:3], kp[t])
                k = ts(P_, P_, sx[:, 3:4], None, MUL, ALU.bypass)
                b = bank()
                for j in range(4):
                    k2 = tr(b.ap[:, 128 * j:128 * j + 128], P_[:, 128 * j:128 * j + 128], k, b.free)
                prf[n] = k2
                cp = copyA if t == 0 else copyV
                b.free = cp(PTb[:, :, 128 * t:128 * t + 128], b.ap.rearrange("p (j n) -> p j n", j=4), k2, ptf2[h % 2])
                toks.append(b.free)
            yield
            b = bank()
            for j in range(4):
                k = mm(b.ap[:, 0:256], vt[:, j, 128 * (h // 4):128 * (h // 4) + 128], PTb[:, j, :], j == 0, j == 3,
                       toks, t_vt, b.free)
            ptf2[h % 2] = k
            oT_tok[h] = b.free = copyA(oT[:, h, :], b.ap[:, 0:256], k, all_n)
            yield

        for _ in weave([head(h) for h in range(8)], 2):
            pass
        tap("oT", oT, oT_tok)
        for q in range(2):
            def add_o(j, p, tok, q=q):
                for i in range(2):
                    c = 4 * q + j + i
                    k = stt(xT[:, c, :], p[:, i, :], mod(1, 2, c, 0), xT[:, c, :], MUL, ADD, tok)
                return k
            t_xa = colproj(load(kcols(a["attn_w_o_2"][0], 512 * q, 512)), oT, oT_tok, add_o)
        tap("xa", xT, t_xa)
        run(ffn(1, 0, xT, hlT, actT, sqb, rsb, cvb, [t_xa, (PE.sem, PE.count), all_n], res))
        yo = f2(qT).rearrange("p (t d) -> p t d", t=2)
        l_out = Line("out")
        for q in range(2):
            for t in range(2):
                b = bank()
                for j in range(4):
                    c = 4 * q + j
                    k = tr(b.ap[:, 128 * j:128 * j + 128], xT[:, c, 128 * t:128 * t + 128], res["tok"], b.free)
                cp = copyA if t == 0 else copyV
                k = b.free = cp(yo[:, t, 512 * q:512 * q + 512], b.ap, k)
                SP.dma(lambda o=out[0, 128 * t:128 * t + 128, 512 * q:512 * q + 512], i=yo[:, t, 512 * q:512 * q + 512]:
                       nc.sync.dma_start(o, i), l_out, k)
        SP.items.append(([(l_out.sem, l_out.count)], None, None, 0))
    if tapl.count:
        SP.items.append(([(tapl.sem, tapl.count)], None, None, 0))

    block = ctx.enter_context(nc.Block())

    @block.sync
    def _(eng):
        tail = [i for i in SP.items if i[1] is None]
        SP.items = [i for i in SP.items if i[1] is not None]
        SP.play(eng)
        for waits, *_ in tail:
            for s, v in waits:
                eng.wait_ge(s, v)

    @block.tensor
    def _(eng):
        PE.play(eng)

    @block.vector
    def _(eng):
        V.play(eng)

    @block.scalar
    def _(eng):
        A.play(eng)

    @block.gpsimd
    def _(eng):
        G.play(eng)

    ctx.close()


_INS = ["x", "norm1_g", "w_in", "conv_w", "gdn_a_log", "gdn_dt_bias", "gdn_norm_g", "mlstm_i_bias",
        "mlstm_f_bias", "mlstm_norm_g", "w_out", "norm2_g", "peer_wq", "peer_keys", "peer_u", "peer_v",
        "normf_g", "c_2", "ctx_2", "c_ctx_2", "ada_w_2", "ada_b_2", "norm_w_2", "pool_w_2", "pool_b_2",
        "pool_scale_2", "attn_w_qkv_2", "attn_q_gain_2", "attn_k_gain_2", "attn_w_o_2", "ffn_w_up_2",
        "ffn_conv_w_2", "ffn_conv_b_2", "ffn_w_down_2"]


def kernel(**inputs):
    import numpy as _np
    import concourse.bacc as _bacc
    from concourse import mybir as _mybir
    from concourse.bass_utils import run_bass_kernel_spmd as _run

    nc = _bacc.Bacc("TRN2", target_bir_lowering=False, num_devices=1)
    arrays, args = {}, {}
    base, levels, late = shape_constants()
    given = {n: inputs[n] for n in _INS} | {"c_base": base, "c_levels": levels, "c_late": late}
    for name, value in given.items():
        v = _np.ascontiguousarray(value)
        arrays[f"in_{name}"] = v
        args[name] = nc.dram_tensor(f"in_{name}", v.shape, _mybir.dt.from_np(v.dtype), kind="ExternalInput").ap()
    out = nc.dram_tensor("out_0", (1, 256, 1024), _mybir.dt.float32, kind="ExternalOutput").ap()
    program(nc, args, out)
    r = _run(nc, [arrays], core_ids=[0])
    return r.results[0]["out_0"]
```

```python
import numpy as np
import concourse.bass as bass
from concourse import mybir
from contextlib import ExitStack


def shape_constants():
    f = np.float32
    i = np.arange(128)
    ident = np.eye(128, dtype=f)
    lo = (i[:, None] <= i[None, :]).astype(f)
    hi = (i[:, None] >= i[None, :]).astype(f)
    one, zero = np.ones((128, 128), f), np.zeros((128, 128), f)
    mask2f = np.concatenate([lo, one, zero, lo], 1)
    mask2b = np.concatenate([hi, zero, one, hi], 1)
    swap = np.zeros((128, 128), f)
    for base in (0, 64):
        for r in range(32):
            swap[base + 32 + r, base + r] = -1.0
            swap[base + r, base + 32 + r] = 1.0
    iota = np.broadcast_to(np.arange(16, dtype=f), (128, 16))
    base = np.concatenate([ident, lo, hi, mask2f, mask2b, swap, iota], 1)
    levels = []
    for d in range(2):
        for l in range(7):
            b = 1 << l
            same = (i[:, None] // (2 * b)) == (i[None, :] // (2 * b))
            first = (i // b) % 2 == 0
            m = same & first[:, None] & ~first[None, :]
            levels.append((m if d == 0 else m.T).astype(f))
    levels = np.concatenate(levels, 1)
    t = np.arange(256)
    inv = np.power(10000.0, -np.arange(0, 64, 2, dtype=np.float32) / 64).astype(f)
    row = (t // 64).astype(f)[:, None] * inv
    col = (t % 64).astype(f)[:, None] * inv
    ang = np.concatenate([row, row, col, col], 1).T
    cnt = []
    for win in (2, 4, 8, 16):
        a = np.clip(t - win // 2, 0, 256)
        b = np.clip(t + win // 2, 0, 256)
        cnt.append((1.0 / (b - a)).astype(f))
    cnt = np.broadcast_to(np.concatenate(cnt), (128, 1024))
    late = np.concatenate([np.cos(ang).astype(f), np.sin(ang).astype(f), cnt], 1)
    return (np.ascontiguousarray(base, f), np.ascontiguousarray(levels, f), np.ascontiguousarray(late, f))


def program(nc, a, out, stop=99, taps=None):
    F32, U32 = mybir.dt.float32, mybir.dt.uint32
    ALU, ACT, AX = mybir.AluOpType, mybir.ActivationFunctionType, mybir.AxisListType
    MUL, ADD, SUB, MAX, MIN = ALU.mult, ALU.add, ALU.subtract, ALU.max, ALU.min
    ctx = ExitStack()
    taps = taps or {}
    PEK, EVERY = 3, 5

    class Queue:
        def __init__(self, name, chained):
            self.sem = ctx.enter_context(nc.semaphore("s_" + name))
            self.count, self.items, self.chained = 0, [], chained

        def __call__(self, fn, *waits, free=False):
            waits = list(flat(waits))
            if self.chained and self.count and not free:
                waits.append((self.sem, self.count))
            self.count += 1
            self.items.append((waits, fn, self.sem, 1))
            return (self.sem, self.count)

        def dma(self, fn, line, *waits):
            line.count += 16
            self.items.append((list(flat(waits)), fn, line.sem, 16))
            return (line.sem, line.count)

        def play(self, eng):
            seen = {}
            for waits, fn, sem, inc in self.items:
                for s, v in waits:
                    if seen.get(id(s), 0) < v:
                        eng.wait_ge(s, v)
                        seen[id(s)] = v
                fn().then_inc(sem, inc)

    class Line:
        def __init__(self, name):
            self.sem, self.count = ctx.enter_context(nc.semaphore("d_" + name)), 0

    def flat(x):
        for t in x:
            if t is None:
                continue
            if isinstance(t, list):
                yield from flat(t)
            else:
                yield t

    PE, V, A, G, SP = Queue("pe", False), Queue("dve", True), Queue("act", True), Queue("pool", True), Queue("sp", False)
    vec, act, pool, pe = nc.vector, nc.scalar, nc.gpsimd, nc.tensor

    def sb(name, n, dt=F32, p=128):
        return ctx.enter_context(nc.sbuf_tensor(name, [p, n], dt))

    def bc(ap, n, at=None):
        v = ap.unsqueeze(len(ap.shape) if at is None else at)
        shape = list(v.shape)
        shape[len(ap.shape) if at is None else at] = n
        return v.broadcast_to(shape)

    cbase = sb("cbase", 128 * 12 + 16)
    ident, lo, hi = cbase[:, 0:128], cbase[:, 128:256], cbase[:, 256:384]
    mask2 = [cbase[:, 384:896], cbase[:, 896:1408]]
    swap, iota16 = cbase[:, 1408:1536], cbase[:, 1536:1552]
    tri = [lo, hi]
    ones = sb("ones", 128)[:, :]
    eps = sb("eps", 1)[:, :]
    cl = sb("cl", 1792)
    cosT, sinT, rcnt = cl[:, 0:256], cl[:, 256:512], cl[:, 512:1536]
    vecT = sb("vecT", 640)
    convw = sb("convw", 60)
    small = sb("small", 64)
    mods = [sb("mods0", 96), sb("mods1", 96)]
    wring = sb("wring", 3 * 4096)
    gt = sb("gt", 340)[:, :]
    ss = sb("ss", 8)[:, :]
    st = sb("st", 48)
    derived = sb("derived", 2 * 2 * 2 * 8 + 2 * 16 + 16)
    rowt = sb("rowt", 3 * 256, p=8)
    ring_buf = sb("rsb", 256)[:, :]
    cvb = [sb(f"cvb{i}", 512)[:, :].rearrange("p (i n) -> p i n", i=2) for i in range(2)]
    early = ExitStack()
    arena = early.enter_context(nc.sbuf_tensor("arena", [128, 29760], F32))
    wring3 = early.enter_context(nc.sbuf_tensor("wring3", [128, 4096], F32))

    class Area:
        def __init__(self, at=0):
            self.at = at

        def take(self, n, dt=None):
            v = arena[:, self.at:self.at + n]
            self.at += n
            assert self.at <= 29760, self.at
            return v if dt is None else v.bitcast(dt)

    class Bank:
        def __init__(self, i):
            t = ctx.enter_context(nc.psum_tensor(f"ps{i}", [128, 512], F32))
            self.ap, self._free, self.held = t[:, :], None, False

        @property
        def free(self):
            return self._free

        @free.setter
        def free(self, token):
            self._free, self.held = token, False

    banks = [Bank(i) for i in range(8)]
    turn, shared = [0], [banks[0:7]]
    bank_ada = banks[7]

    def bank():
        for _ in range(8):
            turn[0] += 1
            b = shared[0][turn[0] % len(shared[0])]
            if not b.held:
                b.held = True
                return b
        raise RuntimeError("every bank is held")

    def run(gen):
        while True:
            try:
                next(gen)
            except StopIteration as e:
                return e.value

    def weave(gens, width):
        gens, live = list(gens), []
        while gens or live:
            while gens and len(live) < width:
                live.append(gens.pop(0))
            for g in list(live):
                try:
                    next(g)
                except StopIteration:
                    live.remove(g)
            yield

    class Slot:
        def __init__(self, i):
            self.ap = wring[:, i * 4096:(i + 1) * 4096] if i < 3 else wring3[:, :]
            self.line, self.ready = Line(f"w{i}"), None
            self._free, self.held = None, False

        @property
        def free(self):
            return self._free

        @free.setter
        def free(self, token):
            self._free, self.held = token, False

    slots = [Slot(i) for i in range(4)]
    wturn = [0]

    def load(*parts):
        s = slots[wturn[0] % len(slots)]
        wturn[0] += 1
        assert not s.held
        s.held = True
        for put, src in parts:
            s.ready = SP.dma(lambda d=put(s.ap), c=src: nc.sync.dma_start(d, c), s.line, s.free)
        return s

    def kcols(w, c0, n):
        return ((lambda ap: ap[:, 0:8 * n].rearrange("p (k c) -> p k c", k=8)),
                w[:, c0:c0 + n].rearrange("(k p) c -> p k c", p=128))

    def mm(o, l, r, start, stop, *waits):
        return PE(lambda: pe.matmul(o, l, r, start=start, stop=stop), *waits)

    def tr(o, i, *waits):
        n = i.shape[0]
        return PE(lambda: pe.transpose(o, i, ident[0:n, 0:n]), *waits)

    def tt(o, x, y, op, *w, eng=None):
        e, n = (G, pool) if eng is G else (V, vec)
        return e(lambda: n.tensor_tensor(o, x, y, op), *w)

    def ts(o, x, s1, s2, op0, op1, *w):
        return V(lambda: vec.tensor_scalar(o, x, s1, s2, op0, op1), *w)

    def stt(o, x, s, y, op0, op1, *w):
        return V(lambda: vec.scalar_tensor_tensor(o, x, s, y, op0, op1), *w)

    def actf(o, x, f, *w, bias=0.0, scale=1.0, accum=None):
        return A(lambda: act.activation(o, x, f, bias=bias, scale=scale, accum_out=accum), *w)

    def copyA(o, x, *w):
        return A(lambda: act.activation(o, x, ACT.Copy), *w)

    def copyV(o, x, *w):
        return V(lambda: vec.tensor_copy(o, x), *w)

    def recip(o, x, *w):
        return V(lambda: vec.reciprocal(o, x), *w)

    tapl = Line("tap")

    def tap(name, ap, *w):
        if name in taps:
            SP.dma(lambda: nc.sync.dma_start(taps[name], ap), tapl, *w)

    l_c, l_x, l_v, l_s = Line("c"), Line("x"), Line("v"), Line("s")

    def ld(o, src, line, *w):
        return SP.dma(lambda: nc.sync.dma_start(o, src), line, *w)

    ar = Area()
    x1 = ar.take(2048).rearrange("p (t d) -> p t d", t=2)
    hT = ar.take(2048).rearrange("p (c n) -> p c n", c=8)
    raw = ar.take(12 * 260).rearrange("p (b n) -> p b n", b=12)
    zT, mqT, mkT, moT = (ar.take(1024).rearrange("p (b n) -> p b n", b=4) for _ in range(4))
    mv = ar.take(1032).rearrange("p (t h e) -> p t h e", t=2, h=4)
    qkv_at = ar.at
    qkv = ar.take(3072).rearrange("p (b n) -> p b n", b=12)
    ktok = ar.take(1024).rearrange("p (t h e) -> p t h e", t=2, h=4)
    vtok = ar.take(1024).rearrange("p (t h e) -> p t h e", t=2, h=4)
    mark = ar.at
    ET, AT, PQ, OT, DD, DT = (ar.take(2048).rearrange("p (m n) -> p m n", m=16) for _ in range(6))

    xv = a["x"][0].rearrange("(t p) d -> p t d", p=128)
    l_x2 = Line("x2")
    t_x = [ld(x1[:, 0, :], xv[:, 0, :], l_x), ld(x1[:, 1, :], xv[:, 1, :], l_x2)]
    t_c = ld(cbase[:, :], a["c_base"], l_c)
    stage = arena[:, qkv_at:qkv_at + 640].rearrange("p (t c) -> p t c", t=5)
    rows = {}
    at = 0

    def vrow(line, name, src, n):
        nonlocal at
        rows[name] = at
        done = 0
        while done < n:
            t, r = divmod(at, 128)
            m = min(n - done, 128 - r)
            tok = ld(stage[r:r + m, t, :], src[done:done + m, :], line)
            at += m
            done += m
        return tok

    def rr(ap):
        return ap.rearrange("(r c) -> r c", c=128)

    for i, nm in enumerate(["gdn_dt_bias", "gdn_a_log", "mlstm_i_bias", "mlstm_f_bias"]):
        src = a[nm][0].rearrange("a h -> (a h)").partition_broadcast(128)
        t_sm = ld(small[:, 8 * i:8 * i + 8], src, l_s)
    sm = small[:, 0:32]
    vrow(l_v, "n1", rr(a["norm1_g"][0]), 8)
    vrow(l_v, "mln", rr(a["mlstm_norm_g"][0]), 4)
    vrow(l_v, "gdn", rr(a["gdn_norm_g"][0]), 1)
    vrow(l_v, "qg", rr(a["attn_q_gain_2"][0]), 1)
    vrow(l_v, "kg", rr(a["attn_k_gain_2"][0]), 1)
    vrow(l_v, "nf", rr(a["normf_g"]), 8)
    vrow(l_v, "c", rr(a["c_2"][0]), 8)
    vrow(l_v, "cc", rr(a["c_ctx_2"]), 8)
    vrow(l_v, "pb", rr(a["pool_b_2"][0]), 8)
    vrow(l_v, "psc", rr(a["pool_scale_2"][0]), 8)
    vrow(l_v, "nw", a["norm_w_2"].rearrange("a b (r c) -> (a b r) c", c=128), 32)
    t_v = vrow(l_v, "adb0", a["ada_b_2"].rearrange("a (r c) -> (a r) c", c=128)[0:41], 41)

    w_in = a["w_in"][0]
    wg = load(kcols(w_in, 2048, 16))
    wg2ap = wg.ap[:, 128:256].rearrange("p (k c) -> p k c", k=8)
    wg.ready = SP.dma(lambda: nc.sync.dma_start(wg2ap, w_in[:, 4112:4128].rearrange("(k p) c -> p k c", p=128)), wg.line)
    w_k, w_v, w_q = load(kcols(w_in, 512, 512)), load(kcols(w_in, 1024, 512)), load(kcols(w_in, 0, 512))
    t_cw = ld(convw[:, :].rearrange("p (b k) -> p b k", b=12),
              a["conv_w"][0].rearrange("(b p) k -> p b k", p=128), l_s)
    l_v2 = Line("v2")
    vrow(l_v2, "adb1", a["ada_b_2"].rearrange("a (r c) -> (a r) c", c=128)[41:96], 55)
    vrow(l_v2, "cw", a["ffn_conv_w_2"].rearrange("a b (r c) -> (a b r) c", c=128), 264)
    t_v2 = vrow(l_v2, "cb", a["ffn_conv_b_2"].rearrange("a (r c) -> (a r) c", c=128), 88)
    rows["adb"] = rows["adb0"]
    t_cl = ld(cl[:, :], a["c_levels"], l_c)
    t_ones = V(lambda: vec.memset(ones, 1.0))
    t_eps = V(lambda: vec.memset(eps, 1e-6))

    def vcol(name, i=0):
        r = rows[name] + i
        return vecT[:, r:r + 1]

    def vcols(name, n):
        return vecT[:, rows[name]:rows[name] + n]

    def vec_cols(t0, t1, tv):
        for t in range(t0, t1):
            n = min(128, at - 128 * t)
            b = bank()
            tk = tr(b.ap[:, 0:n], stage[0:n, t, :], t_c, tv, b.free)
            k = b.free = copyA(vecT[:, 128 * t:128 * t + n], b.ap[:, 0:n], tk)
        return k, tk

    def token_norm(xt, toks, tmp, ss, out):
        res = []
        for t in range(2):
            s = ss[:, 4 * t:4 * t + 4]
            k = actf(tmp[:, 0:1024], xt[:, t, :], ACT.Square, toks[t], t_eps, accum=s[:, 0:1])
            k = actf(s[:, 1:2], s[:, 0:1], ACT.Sqrt, k, bias=eps, scale=1.0 / 1024)
            k = recip(s[:, 2:3], s[:, 1:2], k)
            res.append(out(t, s[:, 2:3], k))
        return res

    def blocks_T(o, xt, t, c0, tok, evac):
        b = bank()
        for j in range(4):
            k = tr(b.ap[:, 128 * j:128 * j + 128], xt[:, 128 * j:128 * j + 128], tok, b.free)
        b.free = evac(o[:, c0:c0 + 4, 128 * t:128 * t + 128], b.ap.rearrange("p (c n) -> p c n", c=4), c0, k)
        return b.free

    def to_cols(o, xt, toks, evac):
        return [blocks_T(o, xt[:, t, 512 * q:512 * q + 512], t, 4 * q, toks[t], evac) for t in range(2) for q in range(2)]

    xn = arena[:, mark:mark + 2048].rearrange("p (t d) -> p t d", t=2)
    tmp1 = arena[:, mark + 2048:mark + 3072]
    t_xn = token_norm(x1, t_x, tmp1, ss,
                      lambda t, r, k: ts(xn[:, t, :], x1[:, t, :], r, None, MUL, ALU.bypass, k))
    t_vec, _ = vec_cols(0, 1, t_v)

    def evac_g(name):
        def f(o, p, c0, tok):
            return tt(o, p, bc(vecT[:, rows[name] + c0:rows[name] + c0 + 4], 128), MUL, tok, t_vec)
        return f

    t_hT = to_cols(hT, xn, [[t_xn[0], t_c], [t_xn[1], t_c]], evac_g("n1"))
    tap("hT", hT, t_hT)
    t_pad = V(lambda: vec.memset(raw[:, :, 0:2], 0.0))
    t_pad = V(lambda: vec.memset(raw[:, :, 258:260], 0.0))
    t_one = V(lambda: vec.memset(mv[:, :, :, 128:129], 1.0))

    def mod(l, part, c, s):
        o = ((part * 8) + c) * 2 + s
        return mods[l][:, o:o + 1]

    AD = derived[:, 0:64].rearrange("p (l q s c) -> p l q s c", l=2, q=2, s=2)
    PG = derived[:, 64:80].rearrange("p (s c) -> p s c", s=2)
    PB = derived[:, 80:96].rearrange("p (s c) -> p s c", s=2)
    sc16 = derived[:, 96:112].rearrange("p (c s) -> p c s", s=2)
    t_mods = [None, None]

    ahead = []
    ada_at = [0]
    NADA = 24

    def ada_load(n=1):
        for _ in range(n):
            if ada_at[0] < NADA:
                l, g = divmod(ada_at[0], 12)
                ada_at[0] += 1
                ahead.append([l, g, load(kcols(a["ada_w_2"][l], 512 * g, 512)), 0])

    def fill(n=4):
        for _ in range(n):
            if not ahead:
                return
            l, g, s, j = ahead[0]
            ahead[0][3] += 1
            w = s.ap.rearrange("p (k c) -> p k c", k=8)
            o = 96 * l + (4 * g + j) * 2
            for kk in range(8):
                k = mm(bank_ada.ap[:, o:o + 2], w[:, kk, 128 * j:128 * j + 128], sc16[:, kk, :], kk == 0,
                       kk == 7, s.ready, t_c16, bank_ada.free)
            if j == 3:
                s.free = ada_done[l] = k
                ahead.pop(0)

    t_c16 = actf(sc16.rearrange("p c s -> p s c"), vecT[:, rows["c"]:rows["c"] + 16].rearrange("p (s c) -> p s c", s=2),
                 ACT.Silu, t_vec)
    ada_done = [None, None]

    def ada_finish(l, q):
        mv_ = mods[l][:, 48 * q:48 * q + 48].rearrange("p (b s) -> p b s", s=2)
        k = tt(mv_, bank_ada.ap[:, 96 * l + 48 * q:96 * l + 48 * q + 48].rearrange("p (b s) -> p b s", s=2),
               bc(vecT[:, rows["adb"] + 48 * l + 24 * q:rows["adb"] + 48 * l + 24 * q + 24], 2), ADD, ada_done[l], t_vec, t_vec2)
        bank_ada.free = k
        for s_ in range(2):
            part = mods[l][:, 16 * (3 * q + 1):16 * (3 * q + 1) + 16].rearrange("p (c s) -> p c s", s=2)[:, :, s_]
            nw = vecT[:, rows["nw"] + 16 * l + 8 * q:rows["nw"] + 16 * l + 8 * q + 8]
            k = stt(AD[:, l, q, s_, :], part, 1.0, nw, ADD, MUL)
        if l == 0 and q == 0:
            for s_ in range(2):
                g1 = mods[0][:, 32:48].rearrange("p (c s) -> p c s", s=2)[:, :, s_]
                k = tt(PG[:, s_, :], g1, vcols("psc", 8), MUL)
                k = tt(PB[:, s_, :], PG[:, s_, :], vcols("pb", 8), MUL)
        t_mods[l] = k

    def ada_rest(l, q):
        end = 12 * l + 6 * q + 6
        while ada_at[0] < end or ahead:
            if ada_at[0] < end and len(ahead) < 2:
                ada_load()
            fill(2)
            yield
        ada_finish(l, q)
        yield

    def colproj(s, rhs, toks, consume, nb=4, width=4):
        w = s.ap[:, 0:8 * 128 * width].rearrange("p (k c) -> p k c", k=8)
        for j in range(0, nb, 2):
            b = bank()
            for i in range(2):
                for kk in range(8):
                    k = mm(b.ap[:, 256 * i:256 * i + 256], w[:, kk, 128 * (j + i):128 * (j + i) + 128],
                           rhs[:, kk, :], kk == 0, kk == 7, s.ready, toks, b.free)
            b.free = consume(j, b.ap.rearrange("p (i n) -> p i n", i=2), k)
            s.free = k
        return b.free

    b = bank()
    gv = b.ap[:, 0:64].rearrange("p (t c) -> p t c", t=2)
    wgv = [wg.ap[:, 0:128].rearrange("p (k c) -> p k c", k=8), wg2ap]
    for t in range(2):
        for i in range(2):
            for kk in range(8):
                k = mm(gv[:, t, 16 * i:16 * i + 16], hT[:, kk, 128 * t:128 * t + 128], wgv[i][:, kk, :],
                       kk == 0, kk == 7, wg.ready, t_hT, b.free)
    wg.free = k
    go = [0]

    def gtake(n):
        go[0] += n
        return gt[:, go[0] - n:go[0]]

    GX = gtake(64).rearrange("p (t c) -> p t c", t=2)
    GU = gtake(32).rearrange("p (t c) -> p t c", t=2)
    GE = gtake(32).rearrange("p (t c) -> p t c", t=2)
    GL = gtake(32).rearrange("p (t c) -> p t c", t=2)
    BETA = gtake(16).rearrange("p (t c) -> p t c", t=2)
    na = gtake(8)
    k = tt(GX[:, :, 0:8], gv[:, :, 0:8], bc(sm[:, 0:8], 2, 1), ADD, k, t_sm)
    k = copyV(GX[:, :, 8:16], gv[:, :, 8:16])
    k = tt(GX[:, :, 16:32], gv[:, :, 16:32], bc(sm[:, 16:32], 2, 1), ADD)
    b.free = k
    k = copyV(GU[:, :, 0:8], GX[:, :, 0:8], k)
    k = ts(GU[:, :, 8:16], GX[:, :, 24:32], -1.0, None, MUL, ALU.bypass)
    k2 = actf(BETA, GX[:, :, 8:16], ACT.Sigmoid, k)
    k = stt(GE, GU, -1.0, GU, MUL, MIN)
    k = actf(GE, GE, ACT.Exp, k)
    k = actf(GE, GE, ACT.Ln, k, bias=ones[:, 0:1])
    k3 = actf(na, sm[:, 8:16], ACT.Exp)
    k = stt(GL, GU, 0.0, GE, MAX, ADD, k)
    k = stt(GL[:, :, 0:8], GL[:, :, 0:8], -1.0, bc(na, 2, 1), MUL, MUL, k3)
    t_gl = ts(GL[:, :, 8:16], GL[:, :, 8:16], -1.0, None, MUL, ALU.bypass, k2)
    tap("GL", GL, t_gl)
    tap("BETA", BETA, t_gl)

    def keep(dst, off=0):
        def f(j, p, tok):
            return copyA(dst[:, off + j:off + j + 2, 2:258] if dst is raw else dst[:, off + j:off + j + 2, :], p, tok)
        return f

    t_raw = [colproj(w_k, hT, t_hT, keep(raw, 4))]

    b = bank()
    for d in range(2):
        for t in range(2):
            o = d * 8 + t * 4
            k = mm(b.ap[:, o:o + 4], tri[d], GL[:, t, 4 * d:4 * d + 4], True, True, t_gl, t_c, t_ones, b.free)
            o += 32
            other = (d == 0 and t == 1) or (d == 1 and t == 0)
            k = mm(b.ap[:, o:o + 4], tri[d], GL[:, t, 8 + 4 * d:12 + 4 * d], True, not other)
            if other:
                k = mm(b.ap[:, o:o + 4], ones, GL[:, 1 - t, 8 + 4 * d:12 + 4 * d], False, True)
    for t in range(2):
        k = mm(b.ap[:, 16 + 8 * t:24 + 8 * t], ones, GL[:, t, 0:8], True, True)
    Gc = gtake(16)
    Fc = gtake(16)
    GT = gtake(16)
    CC = gtake(16)
    bt = gtake(16)
    NBE = gtake(16)
    EG = gtake(16)
    EM = gtake(16)
    hdt = lambda ap: ap.rearrange("p (h d t) -> p d t h", h=4, d=2)
    psv = lambda o: b.ap[:, o:o + 16].rearrange("p (d t h) -> p d t h", d=2, t=2)
    k = V(lambda o=hdt(Gc), i=psv(0): vec.tensor_copy(o, i), k)
    k = V(lambda o=Fc.rearrange("p (t d h) -> p d t h", t=2, d=2), i=psv(32): vec.tensor_copy(o, i))
    gtot = b.ap[:, 16:32].rearrange("p (t d h) -> p d t h", t=2, d=2)
    k = tt(hdt(GT), gtot, hdt(Gc), SUB)
    b.free = k
    k = tt(CC.rearrange("p (t c) -> p t c", t=2), GX[:, :, 16:24], Fc.rearrange("p (t c) -> p t c", t=2), SUB)
    k = copyV(hdt(bt), BETA.rearrange("p t (d h) -> p d t h", d=2))
    kE = actf(EG, Gc, ACT.Exp, k)
    kE = actf(GT, GT, ACT.Exp)
    t_cols = stt(NBE, EG, -1.0, bt, MUL, MUL, kE)

    crow, mf, mb = rowt[:, 0:256], rowt[:, 256:512], rowt[:, 512:768]
    b = bank()
    for t in range(2):
        k = tr(b.ap[0:8, 128 * t:128 * t + 128], CC[:, 8 * t:8 * t + 8], t_cols, b.free)
    k = copyV(crow, b.ap[0:8, 0:256], k)
    b.free = k
    k = V(lambda: vec.tensor_tensor_scan(mf, crow, crow, 0.0, MAX, MAX), k)
    k = V(lambda: vec.tensor_tensor_scan(mb[:, ::-1], crow[:, ::-1], crow[:, ::-1], 0.0, MAX, MAX), k)
    k = ts(rowt[:, 256:768], rowt[:, 256:768], -1.0, None, MUL, ALU.bypass)
    t_rows = k
    t_raw.append(colproj(w_v, hT, t_hT, keep(raw, 8)))
    b = bank()
    for d, r in ((0, mf), (1, mb)):
        for t in range(2):
            o = 16 * d + 8 * t
            kk = tr(b.ap[:, o:o + 8], r[:, 128 * t:128 * t + 128], k, b.free)
    for d in range(2):
        k = tt(EM.rearrange("p (h d t) -> p d t h", h=4, d=2)[:, d], b.ap[:, 16 * d:16 * d + 16]
               .rearrange("p (t c) -> p t c", t=2)[:, :, 4 * d:4 * d + 4],
               Fc.rearrange("p (t c) -> p t c", t=2)[:, :, 4 * d:4 * d + 4], SUB, kk)
    b.free = k
    t_em = actf(EM, EM, ACT.Exp, k)

    def conv(g, tk):
        taps0 = []
        for blk in range(4 * g, 4 * g + 4):
            taps0.append(actf(qkv[:, blk, :], raw[:, blk, 0:256], ACT.Copy, tk, t_pad, t_cw, t_stage,
                              scale=convw[:, 5 * blk:5 * blk + 1]))
        for blk in range(4 * g, 4 * g + 4):
            o, k = qkv[:, blk, :], taps0[blk - 4 * g]
            for j in range(1, 5):
                k = stt(o, raw[:, blk, j:j + 256], convw[:, 5 * blk + j:5 * blk + j + 1], o, MUL, ADD, k)
        return actf(qkv[:, 4 * g:4 * g + 4, :], qkv[:, 4 * g:4 * g + 4, :], ACT.Silu, k)

    t_vec2, t_stage = vec_cols(1, 5, t_v2)
    hm = lambda buf, h: buf[:, 4 * h:4 * h + 4, :]
    f2 = lambda ap: ap.rearrange("p m n -> p (m n)")
    t_et = []

    def decays(h):
        bg = bank()
        for d in range(2):
            for t in range(2):
                o = 128 * (2 * d + t)
                k = mm(bg.ap[:, o:o + 128], bc(GL[:, t, 4 * d + h], 128), tri[d], True, True, t_gl, bg.free)
        br = bank()
        for d in range(2):
            for t in range(2):
                o = 128 * (2 * d + t)
                k2 = mm(br.ap[:, o:o + 128], bc(BETA[:, t, 4 * d + h], 128), ident, True, True, t_gl, br.free)
        for m in range(4):
            kx = ts(ET[:, 4 * h + m, :], bg.ap[:, 128 * m:128 * m + 128], Gc[:, 4 * h + m:4 * h + m + 1], 0.0,
                    SUB, MIN, k, t_cols, t_hT)
        bg.free = kx
        kx = actf(f2(hm(ET, h)), f2(hm(ET, h)), ACT.Exp, kx)
        kb = br.free = tt(f2(hm(AT, h)), f2(hm(ET, h)), br.ap, MUL, kx, k2, t_hT)
        t_et.append([kx, kb])

    t_raw.append(colproj(w_q, hT, t_hT, keep(raw, 0)))
    decays(0)
    decays(1)
    cvt, t_l2 = {}, {}
    cvt[1] = conv(1, t_raw[0])
    s = load(kcols(w_in, 3088, 512))
    w = s.ap.rearrange("p (k c) -> p k c", k=8)
    for t in range(2):
        b = bank()
        for kk in range(8):
            k = mm(b.ap, hT[:, kk, 128 * t:128 * t + 128], w[:, kk, :], kk == 0, kk == 7, s.ready, t_hT, b.free)
        t_mv = b.free = copyA(mv[:, t, :, 0:128], b.ap.rearrange("p (h e) -> p h e", h=4), k)
    s.free = k
    decays(2)
    decays(3)
    sqt = f2(OT).rearrange("p (b n) -> p b n", b=8)
    rq = f2(DD).rearrange("p (b n) -> p b n", b=8)

    def l2(g):
        kq = actf(sqt[:, 4 * g:4 * g + 4, :], qkv[:, 4 * g:4 * g + 4, :], ACT.Square, cvt[g])
        parts = []
        for i in range(2):
            c = 4 * g + 2 * i
            b = bank()
            k = mm(b.ap, ones, sqt[:, c:c + 2, :], True, True, kq, b.free)
            parts.append((c, b, k))
        for c, b, k in parts:
            k = b.free = actf(rq[:, c:c + 2, :], b.ap.rearrange("p (i n) -> p i n", i=2), ACT.Sqrt, k, bias=eps)
            k = recip(rq[:, c:c + 2, :], rq[:, c:c + 2, :], k)
            k = stt(qkv[:, c:c + 2, :], qkv[:, c:c + 2, :], (128 ** -0.5, 1.0)[g], rq[:, c:c + 2, :], MUL, MUL)
        return k

    t_q = colproj(load(kcols(w_in, 2064, 512)), hT, t_hT, keep(mqT))
    cvt[2] = conv(2, t_raw[1])
    t_l2[1] = l2(1)
    t_k = colproj(load(kcols(w_in, 2576, 512)), hT, t_hT, keep(mkT))
    cvt[0] = conv(0, t_raw[2])

    QT, KT = qkv[:, 0:4, :], qkv[:, 4:8, :]
    t_at, t_pq = [None] * 4, [None] * 4
    four = lambda ap: ap.rearrange("p (d t) n -> p d (t n)", d=2)

    def tokens_of(src, dst, tok):
        for t in range(2):
            b = bank()
            for h in range(4):
                k = tr(b.ap[:, 128 * h:128 * h + 128], qkv[:, src + h, 128 * t:128 * t + 128], tok, b.free)
            k = b.free = copyA(dst[:, t], b.ap.rearrange("p (h e) -> p h e", h=4), k)
        return k

    for h in range(4):
        bk = bank()
        for t in range(2):
            sl = slice(128 * t, 128 * t + 128)
            k = mm(bk.ap[:, 128 * t:128 * t + 128], KT[:, h, sl], KT[:, h, sl], True, True, t_l2[1], bk.free)
        t_at[h] = bk.free = tt(four(hm(AT, h)), four(hm(AT, h)), bc(bk.ap[:, 0:256], 2, 1), MUL, k, t_et[h])
    t_l2[0] = l2(0)
    t_z = colproj(load(kcols(w_in, 1536, 512)), hT, t_hT,
                  lambda j, p, tok: actf(zT[:, j:j + 2, :], p, ACT.Silu, tok))

    def level(l, dst, free):
        out = []
        for h in range(4):
            for d in range(2):
                msk = cl[:, 128 * (7 * d + l):128 * (7 * d + l) + 128]
                m = 4 * h + 2 * d
                k = tt(dst[:, m:m + 2, :], AT[:, m:m + 2, :], bc(msk, 2, 1), MUL, t_at[h], t_cl, free[h], eng=G)
            out.append(k)
        return out

    raw2 = arena[:, 4096:6144].rearrange("p (m n) -> p m n", m=16)
    OTs = [OT, raw2]
    X = ET
    sq_done = [t_l2[0], (PE.sem, PE.count)]
    k0 = level(0, OT, [t_l2[0]] * 4)
    t_ktok = tokens_of(4, ktok, t_l2[1])
    t_vtok = tokens_of(8, vtok, cvt[2])
    tap("ktok", ktok, t_ktok)
    t_tok = [t_ktok, t_vtok]
    kdt = []
    for h in range(4):
        bk = bank()
        for t in range(2):
            sl = slice(128 * t, 128 * t + 128)
            k = mm(bk.ap[:, 128 * t:128 * t + 128], KT[:, h, sl], QT[:, h, sl], True, True, t_l2[0], t_l2[1], bk.free)
        kk2 = bk.free = tt(four(hm(PQ, h)), four(hm(ET, h)), bc(bk.ap[:, 0:256], 2, 1), MUL, k, t_et[h])
        kdt.append(kk2)
    t_o = colproj(load(kcols(w_in, 3600, 512)), hT, t_hT,
                  lambda j, p, tok: actf(moT[:, j:j + 2, :], p, ACT.Sigmoid, tok))
    pe_proj = (PE.sem, PE.count)
    loaded = [load(kcols(a["w_out"][0], 0, 512)), load(kcols(a["w_out"][0], 512, 512)),
              load((lambda ap: ap[:, 0:2048].rearrange("p (g d) -> p g d", g=16),
                    a["peer_keys"][0].rearrange("h q k d -> k (h q) d"))),
              load(kcols(a["peer_wq"][0], 0, 512))]
    for h in range(4):
        kd0 = tt(hm(DT, h), bc(ident, 4, 1), hm(OT, h), SUB, k0[h])
        kdt[h] = [kd0, kdt[h]]
    lev_ok = {}
    lev_free = [[kdt[h] for h in range(4)], [[t_raw, cvt[0], cvt[1], cvt[2], (V.sem, V.count)]] * 4]
    lev_ok[1] = level(1, OTs[1], lev_free[1])

    kd = []
    for h in range(4):
        b = bank()
        for i in range(4):
            kk = tr(b.ap[:, 128 * i:128 * i + 128], DT[:, 4 * h + i, :], kdt[h], b.free)
        b.free = copyA(hm(DD, h), b.ap.rearrange("p (m n) -> p m n", m=4), kk)
        kd.append([b.free, kdt[h]])

    def head_level(l, h):
        O = OTs[l % 2]
        b = bank()
        for i in range(4):
            m = 4 * h + i
            k = mm(b.ap[:, 128 * i:128 * i + 128], O[:, m, :], DD[:, m, :], True, True, lev_ok[l][h], kd[h], b.free)
        kO = k
        kx = b.free = copyA(f2(hm(X, h)), b.ap, k, kdt[h])
        yield
        b = bank()
        for i in range(4):
            m = 4 * h + i
            k = mm(b.ap[:, 128 * i:128 * i + 128], X[:, m, :], DT[:, m, :], True, True, kx, b.free)
        if l < 6:
            b2 = bank()
            for i in range(4):
                m = 4 * h + i
                k2 = mm(b2.ap[:, 128 * i:128 * i + 128], DT[:, m, :], X[:, m, :], True, True, b2.free)
            kd2 = b2.free = tt(f2(hm(DD, h)), f2(hm(DD, h)), b2.ap, SUB, k2)
        else:
            kd2 = k
        kd1 = b.free = tt(f2(hm(DT, h)), f2(hm(DT, h)), b.ap, SUB, k, kd2)
        kd[h] = [kd1, kd2]
        head_level.o[l % 2][h] = kO
        yield

    head_level.o = [[None] * 4, [None] * 4]

    SC = 128 ** -0.5
    PTs = [arena[:, 2048 + 512 * i:2560 + 512 * i] for i in range(4)]
    Ym = arena[:, 6144:7168].rearrange("p (t c) -> p t c", t=2)
    ptfree = [pe_proj] * 4
    dns = gtake(16)
    ym_tok = [None] * 8

    def mlstm_head(h):
        bs = bank()
        for J in range(2):
            k_s = mm(bs.ap[:, 256 * J:256 * J + 256], mkT[:, h, 128 * J:128 * J + 128], mqT[:, h, :], True, True,
                     t_q, t_k, bs.free)
        brs = []
        for d in range(2):
            br = bank()
            brs.append((br, mm(br.ap[:, 0:256], bc(ident[0:8, 4 * d + h], 128), (mf, mb)[d], True, True, t_rows, t_em, br.free)))
        yield
        for d in range(2):
            r = 4 * d + h
            n = 2 * h + d
            P_ = PTs[n % 4]
            dn = dns[:, 4 * (n % 4):4 * (n % 4) + 4]
            br, kr = brs[d]
            for J in range(2):
                kp = ts(P_[:, 256 * J:256 * J + 256], br.ap[:, 0:256], CC[:, 8 * J + r:8 * J + r + 1], 0.0, ADD, MIN,
                        kr, ptfree[n % 4])
            br.free = kp
            kp = actf(P_, P_, ACT.Exp, kp)
            yield
            kp = stt(P_, P_, SC, bs.ap, MUL, MUL, kp, k_s)
            if d == 1:
                bs.free = kp
            kp = tt(P_, P_, mask2[d], MUL, kp)
            bo = bank()
            for t in range(2):
                js = {(0, 0): [0], (0, 1): [0, 1], (1, 0): [0, 1], (1, 1): [1]}[(d, t)]
                for J in js:
                    k = mm(bo.ap[:, 129 * t:129 * t + 129], P_[:, 256 * J + 128 * t:256 * J + 128 * t + 128],
                           mv[:, J, h, :], J == js[0], J == js[-1], kp, t_mv, t_one, bo.free)
            ptfree[n % 4] = k
            yield
            ob = bo.ap[:, 0:258].rearrange("p (t e) -> p t e", t=2)
            k = stt(dn[:, 0:2], ob[:, :, 128], -1.0, EM[:, 4 * h + 2 * d:4 * h + 2 * d + 2], MUL, MAX, k, t_em)
            k = tt(dn[:, 0:2], dn[:, 0:2], ob[:, :, 128], MAX)
            k = recip(dn[:, 2:4], dn[:, 0:2])
            for t in range(2):
                yo = Ym[:, t, 128 * h:128 * h + 128]
                if d == 0:
                    k = ts(yo, ob[:, t, 0:128], dn[:, 2 + t:3 + t], None, MUL, ALU.bypass, t_raw)
                else:
                    k = stt(yo, ob[:, t, 0:128], dn[:, 2 + t:3 + t], yo, MUL, ADD)
            bo.free = k
            ym_tok[n] = k
        yield

    def mlstm():
        for h in range(4):
            yield from mlstm_head(h)

    ml = mlstm()
    for l in range(1, 7):
        if l == 1:
            for h in range(4):
                for d in range(2):
                    t_pq[h] = tt(PQ[:, 4 * h + 2 * d:4 * h + 2 * d + 2, :], PQ[:, 4 * h + 2 * d:4 * h + 2 * d + 2, :],
                                 bc(tri[d], 2, 1), MUL, kdt[h], eng=G)
        if l > 1:
            lev_ok[l] = level(l, OTs[l % 2], lev_free[l % 2])
        hs = [head_level(l, h) for h in range(4)]
        for part in range(2):
            for h in range(4):
                next(hs[h], None)
                if (2 * h + part) % 3 != 0:
                    next(ml, None)
        lev_free[l % 2] = list(head_level.o[l % 2])
    run(ml)
    t_T = kd
    tap("DT", DT, t_T)
    pe_T = (PE.sem, PE.count)

    BV = AT
    kb = [None] * 4
    for h in range(4):
        for d in range(2):
            kb[h] = tt(BV[:, 4 * h + 2 * d:4 * h + 2 * d + 2, :], vtok[:, :, h, :],
                       bc(bt[:, 4 * h + 2 * d:4 * h + 2 * d + 2], 128), MUL, lev_ok[6], t_tok, eng=G)
    KD = X
    kkd = None
    for h in range(4):
        for d in range(2):
            m = 4 * h + 2 * d + d
            kkd = ts(KD[:, 2 * h + d, :], ktok[:, d, h, :], GT[:, m:m + 1], None, MUL, ALU.bypass, t_T, pe_T)
    VN = DD
    S1 = X[:, 8:16, :]
    vn_of = lambda d, t: VN.rearrange("p (h e) n -> p e h n", h=4)[:, 2 * d + t]
    quad = lambda b: b.ap.rearrange("p (h n) -> p h n", h=4)
    kv, ks, QS = {}, [None] * 2, [None] * 2

    def state(d):
        b = bank()
        for h in range(4):
            m = 4 * h + 2 * d + d
            k = mm(b.ap[:, 128 * h:128 * h + 128], DT[:, m, :], BV[:, m, :], True, True, t_T, kb, kkd, b.free)
        kv[d, d] = b.free = copyA(vn_of(d, d), quad(b), k, pe_T)
        yield
        b = bank()
        for h in range(4):
            m = 4 * h + 2 * d + d
            k = mm(b.ap[:, 128 * h:128 * h + 128], KD[:, 2 * h + d, :], VN[:, m, :], True, True, kv[d, d], b.free)
        ks[d] = b.free = copyA(S1.rearrange("p (h e) n -> p e h n", h=4)[:, d], quad(b), k)
        yield
        u = 1 - d
        b = bank()
        for h in range(4):
            k = mm(b.ap[:, 128 * h:128 * h + 128], KT[:, h, 128 * u:128 * u + 128], S1[:, 2 * h + d, :], True, True,
                   ks[d], b.free)
        for h in range(4):
            m = 4 * h + 2 * d + u
            kr = stt(BV[:, m, :], b.ap[:, 128 * h:128 * h + 128], NBE[:, m:m + 1], BV[:, m, :], MUL, ADD, k)
        b.free = kr
        yield
        b = bank()
        for h in range(4):
            k = mm(b.ap[:, 128 * h:128 * h + 128], QT[:, h, 128 * u:128 * u + 128], S1[:, 2 * h + d, :], True, True, b.free)
        QS[d] = (b, k)
        b2 = bank()
        for h in range(4):
            m = 4 * h + 2 * d + u
            k = mm(b2.ap[:, 128 * h:128 * h + 128], DT[:, m, :], BV[:, m, :], True, True, kr, b2.free)
        kv[d, u] = b2.free = copyA(vn_of(d, u), quad(b2), k)
        yield

    for _ in weave([state(0), state(1)], 2):
        pass
    Yg = arena[:, mark + 6144:mark + 7168].rearrange("p (t c) -> p t c", t=2)
    yT = arena[:, mark:mark + 2048].rearrange("p (c n) -> p c n", c=8)
    ysq = arena[:, mark + 7168:mark + 8192]
    yrs = gt[:, 0:16]

    def evac_y(o, p, c0, tok, t):
        sl = slice(128 * t, 128 * t + 128)
        if c0 == 0:
            return stt(o, p, vcol("gdn"), zT[:, :, sl], MUL, MUL, tok, t_z, t_vec)
        k = tt(o, p, moT[:, :, sl], MUL, tok, t_o)
        return tt(o, o, bc(vcols("mln", 4), 128), MUL)

    def head_norm_T(Y, t, c0, tok, free):
        sq = ysq[:, 0:512] if c0 == 0 else ysq[:, 512:1024]
        rs = yrs[:, (c0 + 4 * t):(c0 + 4 * t) + 4] if c0 == 0 else yrs[:, 8 + 4 * t:12 + 4 * t]
        y = Y[:, t, :]
        k = tt(sq, y, y, MUL, tok, pe_T)
        k = V(lambda: vec.tensor_reduce(rs, sq.rearrange("p (h e) -> p h e", h=4), AX.X, ADD))
        k = actf(rs, rs, ACT.Sqrt, k, bias=eps, scale=1.0 / 128)
        yield
        k = recip(rs, rs, k)
        yv = y.rearrange("p (h e) -> p h e", h=4)
        k = tt(yv, yv, bc(rs, 128), MUL)
        yield
        head_norm_T.done.append(blocks_T(yT, y, t, c0, [k, free], lambda o, p, c, tk: evac_y(o, p, c, tk, t)))

    head_norm_T.done = []
    x_free = [(PE.sem, PE.count)]

    def gdn_out(t):
        b = bank()
        for h in range(4):
            for d in range(2):
                m = 4 * h + 2 * d + t
                k = mm(b.ap[:, 128 * h:128 * h + 128], PQ[:, m, :], VN[:, m, :], d == 0, d == 1, kv[d, t], t_pq, b.free)
        kc = b.free = copyA(Yg[:, t, :], b.ap, k, pe_T)
        d = 1 - t
        bq, kq = QS[d]
        yield
        for h in range(4):
            m = 4 * h + 2 * d + t
            ky = stt(Yg[:, t, 128 * h:128 * h + 128], bq.ap[:, 128 * h:128 * h + 128], EG[:, m:m + 1],
                     Yg[:, t, 128 * h:128 * h + 128], MUL, ADD, kc, kq)
        bq.free = ky
        yield from head_norm_T(Yg, t, 0, ky, x_free)

    for _ in weave([gdn_out(0), gdn_out(1), head_norm_T(Ym, 0, 4, ym_tok, x_free), head_norm_T(Ym, 1, 4, ym_tok, x_free)], 4):
        pass
    t_yT = head_norm_T.done
    tap("yT", yT, t_yT)
    lev_last = list(lev_ok[6])
    g2b = cl[:, 0:1024]
    l_g2 = Line("g2")
    t_g2 = ld(g2b, a["norm2_g"][0].partition_broadcast(128), l_g2, lev_last)
    t_x1 = [[], []]
    for half in range(2):
        s = loaded[half]
        w = s.ap.rearrange("p (k c) -> p k c", k=8)
        for t in range(2):
            b = bank()
            for kk in range(8):
                k = mm(b.ap, yT[:, kk, 128 * t:128 * t + 128], w[:, kk, :], kk == 0, kk == 7, s.ready, t_yT, b.free)
            xo = x1[:, t, 512 * half:512 * half + 512]
            b.free = tt(xo, xo, b.ap, ADD, k)
            t_x1[t].append(b.free)
        s.free = k
        loaded.append(load(kcols(a["peer_wq"][0], 512 * (half + 1), 512)))
    tap("x1", x1, t_x1)

    NR = 5
    ar = Area(2048)
    h2 = ar.take(2048).rearrange("p (t d) -> p t d", t=2)
    sco = ar.take(4096).rearrange("p (t g n) -> p t g n", t=2, g=16)
    ring = ar.take(2 * NR * 1024).rearrange("p (s d) -> p s d", s=2 * NR)
    own = ar.at
    xcT = ar.take(2048).rearrange("p (c n) -> p c n", c=8)
    hcT = ar.take(2048).rearrange("p (c n) -> p c n", c=8)
    actT = ar.take(22 * 256).rearrange("p (b n) -> p b n", b=22)
    pt = ar.take(1250)
    end1 = [(PE.sem, PE.count), (V.sem, V.count), (A.sem, A.count), (G.sem, G.count)]
    h2T = arena[:, own:own + 2048].rearrange("p (c n) -> p c n", c=8)
    qryT = [arena[:, own + 2048 + 1024 * i:own + 3072 + 1024 * i].rearrange("p (g n) -> p g n", g=4) for i in range(2)]
    keyT = arena[:, own + 4096:own + 6144].rearrange("p (g n) -> p g n", g=16)
    tmpA = arena[:, own + 6144:own + 7168]
    s = loaded[2]
    kv_ = s.ap[:, 0:2048].rearrange("p (g d) -> p g d", g=16)
    for g in range(0, 16, 4):
        b = bank()
        for i in range(4):
            k = tr(b.ap[:, 128 * i:128 * i + 128], kv_[:, g + i, :], s.ready, b.free)
        t_key = b.free = copyA(keyT[:, g:g + 4, :], b.ap.rearrange("p (i n) -> p i n", i=4), k, end1)
    s.free = k
    t_h2 = token_norm(x1, [[t_x1[0], end1], [t_x1[1], end1]], tmpA, ss,
                      lambda t, r, k: stt(h2[:, t, :], x1[:, t, :], r, g2b, MUL, MUL, k, t_g2, end1))
    t_h2T = to_cols(h2T, h2, t_h2, lambda o, p, c0, tok: copyA(o, p, tok, end1))
    t_sco = []
    qfree = [None, None]

    def queries(q):
        s = loaded[3 + q] if q < 3 else load(kcols(a["peer_wq"][0], 512 * q, 512))
        Q = qryT[q % 2]
        w = s.ap.rearrange("p (k c) -> p k c", k=8)
        for j in (0, 2):
            b = bank()
            for i in range(2):
                for kk in range(8):
                    k = mm(b.ap[:, 256 * i:256 * i + 256], w[:, kk, 128 * (j + i):128 * (j + i) + 128],
                           h2T[:, kk, :], kk == 0, kk == 7, s.ready, t_h2T, b.free)
            k = b.free = copyA(Q[:, j:j + 2, :], b.ap.rearrange("p (i n) -> p i n", i=2), k, qfree[q % 2])
            yield
        s.free = (PE.sem, PE.count)
        both = []
        for t in range(2):
            b = bank()
            for i in range(4):
                g = 4 * q + i
                kk = mm(b.ap[:, 128 * i:128 * i + 128], Q[:, i, 128 * t:128 * t + 128], keyT[:, g, :], True, True,
                        k, t_key, b.free)
            b.free = copyA(sco[:, t, 4 * q:4 * q + 4, :], b.ap.rearrange("p (i n) -> p i n", i=4), kk, end1)
            both.append(b.free)
        qfree[q % 2] = kk
        t_sco.append(both)
        yield

    run(queries(0))
    tap("h2", h2, t_h2)

    po = [0]

    def pk(n, dt=None):
        po[0] += n
        assert po[0] <= 1250
        v = pt[:, po[0] - n:po[0]]
        return v if dt is None else v.bitcast(dt)

    top = pk(32)
    topi = pk(32, U32)
    topf = pk(32)
    cand = pk(256)
    best = pk(16)
    posu = pk(16, U32)
    ij = pk(32, U32)
    ijf = pk(32)
    oh = pk(512)
    selv = pk(32)
    idf = pk(16)
    idx = [pk(16, U32) for _ in range(3)]
    dots = [pk(16), pk(16)]
    nmx = pk(1)
    exs = [pk(16), pk(16)]
    ssm = [pk(2), pk(2)]
    gl = pk(16)
    wt = [pk(16), pk(16)]
    LOW = -3.0e38
    last_use = [None] * 3
    hts = [(t, h) for t in range(2) for h in range(8)]
    gate_read = [None, None]

    def topk(i):
        t, h = hts[i]
        for p in range(2):
            sc = sco[:, t, 2 * h + p, :]
            for r in range(2):
                o = slice(16 * p + 8 * r, 16 * p + 8 * r + 8)
                V(lambda o=top[:, o], s=sc: vec.max(o, s), t_sco[h // 2][t], end1)
                V(lambda o=topi[:, o], m=top[:, o], s=sc: vec.max_index(o, m, s))
                if r == 0:
                    V(lambda m=top[:, o], s=sc: vec.match_replace(s, m, s, LOW))
            yield
        copyV(topf, topi)
        cv = cand.rearrange("p (a b) -> p a b", a=16)
        tt(cv, bc(top[:, 0:16], 16), bc(top[:, 16:32], 16, 1), ADD)
        V(lambda: vec.max(best[:, 0:8], cand), topk.best_read)
        V(lambda: vec.max_index(posu[:, 0:8], best[:, 0:8], cand))
        yield
        V(lambda: vec.match_replace(cand, best[:, 0:8], cand, LOW))
        V(lambda: vec.max(best[:, 8:16], cand))
        k = V(lambda: vec.max_index(posu[:, 8:16], best[:, 8:16], cand))
        kn = ts(nmx, best[:, 0:1], -1.0, None, MUL, ALU.bypass)
        ke = topk.best_read = actf(exs[i % 2], best, ACT.Exp, kn, gate_read[i % 2], bias=nmx, accum=ssm[i % 2][:, 0:1])
        yield
        ts(ij[:, 0:16], posu, 4, None, ALU.logical_shift_right, ALU.bypass)
        ts(ij[:, 16:32], posu, 15, None, ALU.bitwise_and, ALU.bypass)
        copyV(ijf, ij)
        ohv = oh.rearrange("p (q a) -> p q a", q=32)
        tt(ohv, bc(ijf, 16), bc(iota16, 32, 1), ALU.is_equal)
        yield
        tt(ohv.rearrange("p (w q) a -> p w q a", w=2), ohv.rearrange("p (w q) a -> p w q a", w=2),
           bc(topf.rearrange("p (w a) -> p w a", w=2), 16, 2), MUL)
        V(lambda: vec.tensor_reduce(selv, ohv, AX.X, ADD))
        stt(idf, selv[:, 0:16], 128.0, selv[:, 16:32], MUL, ADD)
        topk.done = copyV(idx[i % 3], idf, last_use[i % 3])
        recip(ssm[i % 2][:, 1:2], ssm[i % 2][:, 0:1], ke)
        yield

    topk.best_read = None
    u_tab, v_tab = a["peer_u"][0], a["peer_v"][0]
    lines = [Line(f"gr{i}") for i in range(2 * NR)]
    rfree = [end1] * (2 * NR)
    rcount = [0, 0]
    vb = [banks[5], banks[6]]
    diag = [cl[:, 1536:1664], cl[:, 1664:1792]]
    dfree = [lev_last, lev_last]
    wtok = [None, None]
    on_pe = lambda k: k % PEK != 0
    ndiag = [0]
    state_v = {}

    def gelu_weights(j):
        kg = actf(gl, dots[j % 2], ACT.Gelu, state_v["dots", j], state_v.get("w", None))
        state_v["gelu", j] = kg

    def weights(j):
        state_v["w"] = gate_read[j % 2] = wtok[j % 2] = stt(
            wt[j % 2], exs[j % 2], ssm[j % 2][:, 1:2], gl, MUL, MUL, state_v["gelu", j], state_v.get(("used", j - 2)))

    def add_pe(j):
        t, h = hts[j]
        for i in range(2):
            k = vb[i].free = tt(x1[:, t, 512 * i:512 * i + 512], x1[:, t, 512 * i:512 * i + 512], vb[i].ap, ADD,
                                state_v["pe", j])

    pe_first = min(k for k in range(16) if on_pe(k))
    pe_last = max(k for k in range(16) if on_pe(k))

    def consume(item):
        kind, j, k, r, tok = item
        t, h = hts[j]
        if kind == "u":
            rfree[r] = V(lambda o=ring[:, r, :], x=h2[:, t, :], c=dots[j % 2][:, k:k + 1]:
                         vec.tensor_tensor_reduce(out=o, in0=o, in1=x, scale=1.0, scalar=0.0,
                                                  op0=MUL, op1=ADD, accum_out=c), tok, state_v.get(("gelu", j - 2)),
                         free=True)
            state_v["dots", j] = rfree[r]
            if k == 15:
                gelu_weights(j)
        elif on_pe(k):
            n = ndiag[0] % 2
            ndiag[0] += 1
            kd_ = actf(diag[n], ident, ACT.Copy, wtok[j % 2], dfree[n], scale=wt[j % 2][:, k:k + 1])
            for i in range(2):
                kp = mm(vb[i].ap, diag[n], ring[:, r, 512 * i:512 * i + 512], k == pe_first, k == pe_last, kd_, tok,
                        vb[i].free)
            dfree[n] = rfree[r] = kp
            state_v["used", j] = [kp, kd_, state_v.get("acc")]
            if k == pe_last:
                state_v["pe", j] = kp
        else:
            rfree[r] = state_v["acc"] = stt(x1[:, t, :], ring[:, r, :], wt[j % 2][:, k:k + 1], x1[:, t, :], MUL, ADD, tok, wtok[j % 2])

    def peer():
        for _ in topk(0):
            yield
        pend = []
        for i in range(17):
            tix = topk.done
            nxt = topk(i + 1) if i + 1 < 16 else iter(())
            steps = []
            for k in range(16):
                if i < 16:
                    steps.append(("u", i, k))
                if i > 0:
                    steps.append(("v", i - 1, k))
            wrote = i == 0
            done = 0
            for kind, j, k in steps:
                r = NR * (kind == "v") + rcount[kind == "v"] % NR
                rcount[kind == "v"] += 1
                tab = u_tab if kind == "u" else v_tab
                tok = G.dma(lambda o=ring[:, r, :], x=idx[j % 3][:, k:k + 1], tb=tab: pool.indirect_dma_start(
                    out=o, out_offset=None, in_=tb, in_offset=bass.IndirectOffsetOnAxis(ap=x, axis=0)),
                    lines[r], tix, rfree[r])
                if kind == "v":
                    last_use[j % 3] = tok
                pend.append((kind, j, k, r, tok))
                done += 1
                if len(pend) >= NR:
                    it = pend.pop(0)
                    if it[0] == "v" and it[1] == i - 1 and not wrote:
                        weights(i - 1)
                        wrote = True
                    consume(it)
                if done % 3 == 0:
                    next(nxt, None)
                yield
            while pend:
                it = pend.pop(0)
                if it[0] == "v" and not wrote:
                    weights(i - 1)
                    wrote = True
                consume(it)
                yield
            for _ in nxt:
                pass
            if i > 0:
                add_pe(i - 1)

    rs_used = [None]

    def modulated(hT_, xT, l, q, s, tok, sqb, rsb, pad=0, xtoks=None, then=None):
        if xtoks:
            sq = [actf(sqb[:, c, :], xT[:, c, :], ACT.Square, xtoks[c], tok, rs_used[0]) for c in range(8)]
        else:
            sq = [actf(sqb, xT, ACT.Square, tok, rs_used[0])] * 8
            yield
        b = bank()
        for c in range(8):
            k2 = mm(b.ap[:, 0:256], ones, sqb[:, c, :], c == 0, c == 7, sq[c], b.free)
        k = b.free = actf(rsb, b.ap[:, 0:256], ACT.Sqrt, k2, bias=eps, scale=1.0 / 1024)
        yield
        recip(rsb, rsb, k)
        toks, out = [], []
        for c in range(8):
            o = hT_[:, c, pad:pad + 256]
            k = stt(o, xT[:, c, :], AD[:, l, q, s, c:c + 1], rsb, MUL, MUL, t_mods[l])
            toks.append(actf(o, o, ACT.Identity, k, bias=mod(l, 3 * q, c, s)))
            if then and c >= 3:
                out.append(then(c - 3, toks[c - 3]))
        if then:
            out += [then(c, toks[c]) for c in (5, 6, 7)]
        rs_used[0] = k
        yield
        return out if then else toks

    def ffn(l, s, xT, hT_, actb, sqb, rsb, cvb, tok, res):
        th = yield from modulated(hT_, xT, l, 1, s, tok, sqb, rsb)
        wu, wd = a["ffn_w_up_2"][l], a["ffn_w_down_2"][l]
        cwc = lambda j, blk: vcol("cw", 132 * l + 44 * j + blk)
        cvf = [None, None]
        wv = lambda ap, i: ap.rearrange("p (k i c) -> p k i c", k=8, i=2)[:, :, i, :]

        def after(blk, b, k):
            cv = cvb[blk % 2]
            for i in range(2):
                kc = actf(cv[:, i, :], b.ap[:, 256 * i:256 * i + 256], ACT.Identity, k, cvf[blk % 2],
                          bias=vcol("cb", 44 * l + blk + 22 * i), scale=cwc(1, blk + 22 * i))
            for i in range(2):
                u = b.ap[:, 256 * i:256 * i + 256]
                kc = stt(cv[:, i, 1:256], u[:, 0:255], cwc(0, blk + 22 * i), cv[:, i, 1:256], MUL, ADD, kc)
                kc = stt(cv[:, i, 0:255], u[:, 1:256], cwc(2, blk + 22 * i), cv[:, i, 0:255], MUL, ADD)
            b.free = kc
            ks_ = actf(cv[:, 0, :], cv[:, 0, :], ACT.Silu, kc)
            cvf[blk % 2] = tt(actb[:, blk, :], cv[:, 0, :], cv[:, 1, :], MUL, ks_, eng=G if res["pool"] else None)
            return cvf[blk % 2]

        late = None
        for g in range(11):
            sl = load((lambda ap: wv(ap, 0), wu[:, 256 * g:256 * g + 256].rearrange("(k p) c -> p k c", p=128)),
                      (lambda ap: wv(ap, 1), wu[:, 2816 + 256 * g:3072 + 256 * g].rearrange("(k p) c -> p k c", p=128)))
            for jb in range(2):
                b = bank()
                for i in range(2):
                    w = wv(sl.ap, i)
                    for kk in range(8):
                        k = mm(b.ap[:, 256 * i:256 * i + 256], w[:, kk, 128 * jb:128 * jb + 128], hT_[:, kk, :],
                               kk == 0, kk == 7, sl.ready, th[kk], b.free)
                sl.free = k
                if late:
                    ka_ = after(*late)
                late = (2 * g + jb, b, k)
                yield
        ka_ = after(*late)
        for half in range(2):
            bs_ = [bank() for _ in range(4)]
            for f0, nf in ((0, 8), (8, 8), (16, 6)):
                sl = load((lambda ap, nf=nf: ap[:, 0:512 * nf].rearrange("p (f c) -> p f c", f=nf),
                           wd[128 * f0:128 * (f0 + nf), 512 * half:512 * half + 512].rearrange("(f p) c -> p f c", p=128)))
                w = sl.ap[:, 0:512 * nf].rearrange("p (f c) -> p f c", f=nf)
                for m in range(4):
                    for f in range(nf):
                        k = mm(bs_[m].ap[:, 0:256], w[:, f, 128 * m:128 * m + 128], actb[:, f0 + f, :],
                               f0 + f == 0, f0 + f == 21, sl.ready, ka_, bs_[m].free)
                    if f0 + nf == 22:
                        c = 4 * half + m
                        bs_[m].free = stt(xT[:, c, :], bs_[m].ap[:, 0:256], mod(l, 5, c, s), xT[:, c, :], MUL, ADD, k)
                        res["tok"] = bs_[m].free
                    yield
                sl.free = k

    def mix_pool(s, xT, hp, s2, s4, rsb, w, tok, wtoks, dmat, rn, xtoks=None, alt=None):
        ta = V(lambda: vec.memset(hp[:, :, 0:8], 0.0), tok)
        ta = V(lambda: vec.memset(hp[:, :, 264:272], 0.0))
        th = yield from modulated(hp, xT, 0, 0, s, tok, dmat, rsb, pad=8, xtoks=xtoks)
        biased = [actf(xT[:, c, :], xT[:, c, :], ACT.Identity, th[c], bias=PB[:, s, c:c + 1]) for c in range(8)]
        toks = []
        for g in (0, 2, 3, 1) if alt else range(4):
            win = (2, 4, 8, 16)[g]
            e = G if alt and g < 2 else None
            a2, a4 = alt if e else (s2, s4)
            c = slice(2 * g, 2 * g + 2)
            H = hp[:, c, :]
            k = tt(a2[:, :, 1:272], H[:, :, 0:271], H[:, :, 1:272], ADD, th[2 * g + 1], ta, tok, eng=e)
            cur = a2
            if win >= 4:
                k = tt(a4[:, :, 2:271], a2[:, :, 1:270], a2[:, :, 3:272], ADD, eng=e)
                cur = a4
            if win >= 8:
                k = tt(a2[:, :, 4:269], a4[:, :, 2:267], a4[:, :, 6:271], ADD, eng=e)
                cur = a2
            if win >= 16:
                k = tt(a4[:, :, 8:265], a2[:, :, 4:261], a2[:, :, 12:269], ADD, eng=e)
                cur = a4
            k = tt(dmat[:, c, :], cur[:, :, 8:264], bc(rcnt[:, 256 * g:256 * g + 256], 2, 1), MUL, t_late[0], eng=e)
            k = tt(dmat[:, c, :], dmat[:, c, :], H[:, :, 8:264], SUB, eng=e)
            b = bank()
            for j in range(2):
                for kk in range(2):
                    kp = mm(b.ap[:, 256 * j:256 * j + 256], w[:, 2 * g + kk, 128 * j:128 * j + 128], dmat[:, 2 * g + kk, :],
                            kk == 0, kk == 1, wtoks, k, b.free)
            toks.append((g, b, kp))
            yield
        blocks = [None] * 8
        for g, b, kp in toks:
            for c in (2 * g, 2 * g + 1):
                kx = blocks[c] = stt(xT[:, c, :], b.ap[:, 256 * (c % 2):256 * (c % 2) + 256], PG[:, s, c:c + 1], xT[:, c, :],
                                     MUL, ADD, kp, biased[c])
            b.free = kx
        rn["tok"], rn["pe"], rn["blocks"] = kx, kp, blocks
        yield

    hp = actT.rearrange("p b n -> p (b n)")
    hpc = hp[:, 0:8 * 272].rearrange("p (c n) -> p c n", c=8)
    s2b = hp[:, 2176:2176 + 544].rearrange("p (c n) -> p c n", c=2)
    s4b = hp[:, 2720:2720 + 544].rearrange("p (c n) -> p c n", c=2)
    ctx_res = {"pool": False}
    t_late = [None]

    def pool_w():
        sl = load((lambda ap: ap[:, 0:2048].rearrange("p (g c) -> p g c", g=8),
                   a["pool_w_2"][0].rearrange("g (k p) c -> p (g k) c", p=128)))
        return sl, sl.ap[:, 0:2048].rearrange("p (g c) -> p g c", g=8)

    def context():
        xin = hp[:, 3584:5632].rearrange("p (t d) -> p t d", t=2)
        for q in range(1, 4):
            yield from queries(q)
        tap("sco", sco, t_sco)
        prep_done = [(PE.sem, PE.count), (A.sem, A.count)]
        lc = Line("ctx")
        t = ld(xin, a["ctx_2"][0].rearrange("(t p) d -> p t d", p=128), lc, prep_done, t_h2)
        t_late[0] = ld(cl[:, 0:1536], a["c_late"], l_c, t_h2)
        yield
        tx = to_cols(xcT, xin, [t, t], lambda o, p, c0, tok: copyA(o, p, tok, prep_done))
        yield
        yield from ada_rest(0, 0)
        yield from ada_rest(0, 1)
        sl, w = pool_w()
        yield from mix_pool(1, xcT, hpc, s2b, s4b, ring_buf, w, tx, sl.ready, hcT, ctx_res)
        sl.free = ctx_res["pe"]
        tap("xc1", xcT, ctx_res["tok"])
        yield from ffn(0, 1, xcT, hcT, actT, hcT, ring_buf, cvb, [ctx_res["tok"], ctx_res["pe"]], ctx_res)
        tap("xc2", xcT, ctx_res["tok"])
        yield from ada_rest(1, 0)
        thc = yield from modulated(hcT, xcT, 1, 0, 1, [ctx_res["tok"], (PE.sem, PE.count)], hcT, ring_buf)
        skv = load(kcols(a["attn_w_qkv_2"][0], 1024, 512))
        wk = skv.ap.rearrange("p (k c) -> p k c", k=8)
        context.kv = []
        b = bank()
        for hk in range(2):
            for kk in range(8):
                k = mm(b.ap[:, 256 * hk:256 * hk + 256], wk[:, kk, 128 * hk:128 * hk + 128], hcT[:, kk, :], kk == 0,
                       kk == 7, skv.ready, thc, b.free)
        k = b.free = copyA(kc_keep, b.ap, k, ctx_res["tok"])
        context.kv.append(k)
        yield
        for t in range(2):
            b = bank()
            for kk in range(8):
                k = mm(b.ap[:, 0:256], hcT[:, kk, 128 * t:128 * t + 128], wk[:, kk, 256:512], kk == 0, kk == 7, b.free)
            skv.free = k
            b.free = copyA(vc_keep[:, t, :], b.ap[:, 0:256], k)
            context.kv.append(b.free)
            yield

    kvc = cbase[:, 384:1408]
    kc_keep = kvc[:, 0:512]
    vc_keep = kvc[:, 512:1024].rearrange("p (t e) -> p t e", t=2)
    shared[0] = banks[0:5] + [banks[7]]
    if stop >= 2:
        g1_, g2_ = peer(), context()
        n, on = 0, True
        while on:
            on = next(g1_, 0) is None
            n += 1
            if n % EVERY == 0:
                next(g2_, None)
        while next(g2_, 1) is None:
            pass
    t_peer = (V.sem, V.count)
    tap("x2", x1, t_peer)
    shared[0] = banks[0:7]
    endp = [t_peer, (PE.sem, PE.count), (A.sem, A.count), (G.sem, G.count)]
    if stop >= 4:
        del slots[3]
        wturn[0] = 0
        early.close()
        FR = mybir.dt.float32r

        def mem(st, name, n):
            return st.enter_context(nc.sbuf_tensor(name, [128, n], F32))

        cols = lambda t: t[:, :].rearrange("p (c n) -> p c n", n=256)
        yo_, xT_, sqb_ = mem(ctx, "yo", 2048), mem(ctx, "xT", 2048), mem(ctx, "sqb", 2048)
        xT, sqb = cols(xT_), cols(sqb_)
        whl = [(mem(ctx, f"wh{i}", 2048), mem(ctx, f"wl{i}", 2048)) for i in range(3)]
        wfree, wnext = [endp] * 3, [0]

        def fence():
            return [(PE.sem, PE.count), (V.sem, V.count), (A.sem, A.count), (G.sem, G.count)]

        def split_weights(src, n, *toks):
            i = wnext[0] % 3
            wnext[0] += 1
            h, l = whl[i]
            shape = lambda ap: ap if len(src.shape) == 2 else ap.rearrange("p (m c) -> p m c", m=src.shape[1])
            k = A(lambda: act.activation(shape(h[:, 0:n].bitcast(FR)), src, ACT.Copy), wfree[i], *toks)
            yield
            k2 = tt(shape(l[:, 0:n].bitcast(FR)), src, shape(h[:, 0:n]), SUB, wfree[i], k)
            return i, [k, k2]

        def split_rows(H, L, c, src, *toks, eng=None, lo_eng=None):
            o = slice(256 * c, 256 * c + 256)
            if eng is G:
                k = G(lambda: pool.tensor_copy(H[:, o].bitcast(FR), src), *toks)
            else:
                k = A(lambda: act.activation(H[:, o].bitcast(FR), src, ACT.Copy), *toks)
            return [k, tt(L[:, o].bitcast(FR), src, H[:, o], SUB, k, *toks, eng=lo_eng or eng)]

        def mm3(o, lhs, rhs, start, stop, *waits):
            r = lambda ap: ap.bitcast(FR)
            mm(o, r(lhs[0]), r(rhs[0]), start, False, *waits)
            mm(o, r(lhs[0]), r(rhs[1]), False, False)
            return mm(o, r(lhs[1]), r(rhs[0]), False, stop)

        def both(pair, a0, a1):
            return pair[0][:, a0:a1], pair[1][:, a0:a1]

        def ffn3(l, xtoks, tok):
            done = []
            wu, wd = a["ffn_w_up_2"][l], a["ffn_w_down_2"][l]
            cwc = lambda j, blk: vcol("cw", 132 * l + 44 * j + blk)
            wv = lambda ap, i: ap.rearrange("p (k i c) -> p k i c", k=8, i=2)[:, :, i, :]
            st_ = ExitStack()
            hx = mem(st_, f"hh{l}", 2048), mem(st_, f"hl{l}", 2048)
            ax = mem(st_, f"ah{l}", 5632), mem(st_, f"al{l}", 5632)
            pieces = [("up", g, jb) for g in range(11) for jb in range(2)]
            pieces += [("dn", half, q) for half in range(2) for q in range(6)]
            cur, ready = [None], {}

            def prepare(i):
                if i >= len(pieces):
                    return
                kind, g, jb = pieces[i]
                if kind == "up":
                    if jb == 0:
                        cur[0] = load(
                            (lambda ap: wv(ap, 0), wu[:, 256 * g:256 * g + 256].rearrange("(k p) c -> p k c", p=128)),
                            (lambda ap: wv(ap, 1), wu[:, 2816 + 256 * g:3072 + 256 * g].rearrange("(k p) c -> p k c", p=128)))
                    n, last = 2048, jb == 1
                    src = cur[0].ap.rearrange("p (m c) -> p m c", m=16)[:, :, 128 * jb:128 * jb + 128]
                else:
                    if jb % 2 == 0:
                        f0, nf = 4 * jb, min(8, 22 - 4 * jb)
                        cur[0] = load((lambda ap, nf=nf: ap[:, 0:512 * nf].rearrange("p (f c) -> p f c", f=nf),
                                       wd[128 * f0:128 * (f0 + nf), 512 * g:512 * g + 512].rearrange("(f p) c -> p f c", p=128)))
                    n, last = (1024 if jb == 5 else 2048), jb % 2 == 1
                    src = cur[0].ap[:, 2048 * (jb % 2):2048 * (jb % 2) + n]
                sl, parts = cur[0], split_weights(src, n, cur[0].ready)
                next(parts)
                yield
                ready[i] = run(parts)
                if last:
                    sl.free = ready[i][1]

            cvf = [None, None]

            def after(blk, b, k):
                cv = cvb[blk % 2]
                for i in range(2):
                    kc = actf(cv[:, i, :], b.ap[:, 256 * i:256 * i + 256], ACT.Identity, k, cvf[blk % 2],
                              bias=vcol("cb", 44 * l + blk + 22 * i), scale=cwc(1, blk + 22 * i))
                hi_part = prepare(blk + 3)
                next(hi_part, None)
                for i in range(2):
                    u = b.ap[:, 256 * i:256 * i + 256]
                    kc = stt(cv[:, i, 1:256], u[:, 0:255], cwc(0, blk + 22 * i), cv[:, i, 1:256], MUL, ADD, kc)
                    kc = stt(cv[:, i, 0:255], u[:, 1:256], cwc(2, blk + 22 * i), cv[:, i, 0:255], MUL, ADD)
                b.free = kc
                for _ in hi_part:
                    pass
                ks_ = actf(cv[:, 0, :], cv[:, 0, :], ACT.Silu, kc)
                ka = tt(cv[:, 0, :], cv[:, 0, :], cv[:, 1, :], MUL, ks_, eng=G)
                cvf[blk % 2] = split_rows(ax[0], ax[1], blk, cv[:, 0, :], ka, old, eng=G)
                return cvf[blk % 2]

            run(prepare(0))
            old = fence()
            th = run(modulated(sqb, xT, l, 1, 0, tok, sqb, ring_buf, xtoks=xtoks,
                               then=lambda c, tk: split_rows(hx[0], hx[1], c, sqb[:, c, :], tk, old, lo_eng=G if c % 2 else None)))
            run(prepare(1))
            run(prepare(2))
            late = None
            for n in range(22):
                b = bank()
                i_, tw = ready[n]
                for i in range(2):
                    for kk in range(8):
                        m = 128 * (2 * kk + i)
                        k = mm3(b.ap[:, 256 * i:256 * i + 256], both(whl[i_], m, m + 128), both(hx, 256 * kk, 256 * kk + 256),
                                kk == 0, kk == 7, tw, th[kk], b.free)
                wfree[i_] = k
                if late:
                    after(*late)
                late = (n, b, k)
            ka_ = after(*late)
            n = 22
            for half in range(2):
                bs_ = [bank() for _ in range(4)]
                for q in range(6):
                    if n > 22:
                        run(prepare(n + 2))
                    i_, tw = ready[n]
                    n += 1
                    nf = 2 if q == 5 else 4
                    for m in range(4):
                        for f in range(nf):
                            F = 4 * q + f
                            k = mm3(bs_[m].ap[:, 0:256], both(whl[i_], 512 * f + 128 * m, 512 * f + 128 * m + 128),
                                    both(ax, 256 * F, 256 * F + 256), F == 0, F == 21, tw, ka_, bs_[m].free)
                        if q == 5:
                            c = 4 * half + m
                            bs_[m].free = stt(xT[:, c, :], bs_[m].ap[:, 0:256], mod(l, 5, c, 0), xT[:, c, :], MUL, ADD, k)
                            done.append(bs_[m].free)
                    wfree[i_] = k
            st_.close()
            return done

        def colproj3(s, hx, th, consume):
            v_ = s.ap.rearrange("p (k c) -> p k c", k=8)
            un = [run(split_weights(v_[:, :, 256 * u:256 * u + 256], 2048, s.ready)) for u in range(2)]
            s.free = un[1][1]
            for u, (i_, tw) in enumerate(un):
                b = bank()
                for i in range(2):
                    for kk in range(8):
                        m = 256 * kk + 128 * i
                        k = mm3(b.ap[:, 256 * i:256 * i + 256], both(whl[i_], m, m + 128), both(hx, 256 * kk, 256 * kk + 256),
                                kk == 0, kk == 7, tw, th[kk], b.free)
                wfree[i_] = k
                b.free = consume(2 * u, b.ap.rearrange("p (i n) -> p i n", i=2), k)
            return b.free

        st_ = ExitStack()
        xn_, hp_ = mem(st_, "xn2", 2048), mem(st_, "hpool", 3264)
        hpc = hp_[:, 0:2176].rearrange("p (c n) -> p c n", c=8)
        s2b = hp_[:, 2176:2720].rearrange("p (c n) -> p c n", c=2)
        s4b = hp_[:, 2720:3264].rearrange("p (c n) -> p c n", c=2)
        xn2 = xn_[:, :].rearrange("p (t d) -> p t d", t=2)
        tn = token_norm(x1, [endp, endp], sqb_[:, :], ss,
                        lambda t, r, k: ts(xn2[:, t, :], x1[:, t, :], r, None, MUL, ALU.bypass, k, endp))
        tx = to_cols(xT, xn2, tn, evac_g("nf"))
        tap("xT", xT, tx)
        res = {"pool": True}
        sl, w = pool_w()
        alt = [xn_[:, 544 * i:544 * i + 544].rearrange("p (c n) -> p c n", c=2) for i in range(2)]
        run(mix_pool(0, xT, hpc, s2b, s4b, ring_buf, w, [endp, (PE.sem, PE.count)], sl.ready, sqb, res,
                     xtoks=[tx[2 + c // 4] for c in range(8)], alt=alt))
        sl.free = res["pe"]
        tap("xp", xT, res["tok"])
        st_.close()
        tf = ffn3(0, res["blocks"], [res["pe"], tx])
        tap("xf0", xT, tf)
        old = fence()
        am = ExitStack()
        hx = mem(am, "ahh", 2048), mem(am, "ahl", 2048)
        qT_, kT_, vt_, oT_, pr, prT = (mem(am, n_, c_) for n_, c_ in (
            ("qT", 2048), ("kT", 1024), ("vt", 1024), ("oT", 2048), ("pr", 2048), ("prT", 2048)))
        qT, oT = cols(qT_), cols(oT_)
        kTt = kT_[:, :].rearrange("p (c n) -> p c n", c=2)
        vt = vt_[:, :].rearrange("p (t e) -> p t e", t=4)
        wqkv = a["attn_w_qkv_2"][0]
        a11 = ada_rest(1, 1)
        s = load(kcols(wqkv, 1024, 512))
        v_ = s.ap.rearrange("p (k c) -> p k c", k=8)
        un = [run(split_weights(v_[:, :, 0:256], 2048, s.ready))]
        th = run(modulated(sqb, xT, 1, 0, 0, None, sqb, ring_buf, xtoks=tf,
                           then=lambda c, tk: split_rows(hx[0], hx[1], c, sqb[:, c, :], tk, old, lo_eng=G if c % 2 else None)))
        un.append(run(split_weights(v_[:, :, 256:512], 2048, s.ready)))
        s.free = un[1][1]
        kcc = copyA(kTt[:, :, 256:512], kc_keep.rearrange("p (c n) -> p c n", c=2), context.kv, old)
        kvv = copyA(vt[:, 2:4, :], vc_keep)
        b = bank()
        i_, tw = un[0]
        for hk in range(2):
            for kk in range(8):
                m = 256 * kk + 128 * hk
                k = mm3(b.ap[:, 256 * hk:256 * hk + 256], both(whl[i_], m, m + 128), both(hx, 256 * kk, 256 * kk + 256),
                        kk == 0, kk == 7, tw, th[kk], b.free)
        wfree[i_] = k
        kb_ = b.free = copyA(kTt[:, :, 0:256], b.ap.rearrange("p (c n) -> p c n", c=2), k)
        i_, tw = un[1]
        for t in range(2):
            b = bank()
            for kk in range(8):
                m = 256 * kk + 128 * t
                k = mm3(b.ap[:, 0:256], both(hx, m, m + 128), both(whl[i_], 256 * kk, 256 * kk + 256), kk == 0, kk == 7, tw, b.free)
            t_vt = b.free = copyA(vt[:, t, :], b.ap[:, 0:256], k)
        wfree[i_] = k
        t_vt = [t_vt, kvv]
        scr = sqb_
        scrs = [(scr[:, 0:512], scr[:, 512:1024], scr[:, 1024:1536]),
                (oT_[:, 0:512], oT_[:, 512:1024], oT_[:, 1024:1536]),
                (prT[:, 0:512], prT[:, 512:1024], prT[:, 1024:1536])]
        sfree = [[old, th]] * 3
        nh = [0]
        hn = {}

        def headnorm(key, x, gain, tok, rope):
            z = nh[0] % 3
            rs = st[:, 32 + 4 * z:36 + 4 * z]
            nh[0] += 1
            sq2, xc, ro = scrs[z]
            k = actf(sq2, x, ACT.Square, tok, sfree[z])
            yield
            b = bank()
            for i in range(4):
                k = mm(b.ap[:, i:i + 1], sq2[:, 128 * i:128 * i + 128], ones[:, 0:1], True, True, k, b.free)
            k = b.free = actf(rs, b.ap[:, 0:4], ACT.Sqrt, k, bias=eps, scale=1.0 / 128)
            k = recip(rs, rs, k)
            yield
            b = bank()
            for i in range(4):
                k2 = mm(b.ap[:, 128 * i:128 * i + 128], bc(rs[:, i], 128), ident, True, True, k, b.free)
            k = b.free = stt(x, x, vcol(gain), b.ap, MUL, MUL, tok, k2)
            yield
            b = bank()
            k2 = mm(b.ap[:, 0:256 * rope], swap, x[:, 0:256 * rope], True, True, k, b.free)
            bv = lambda ap: ap.rearrange("p (i n) -> p i n", i=rope)
            xr = x[:, 0:256 * rope]
            kg = tt(bv(xc[:, 0:256 * rope]), bv(xr), bc(cosT, rope, 1), MUL, k, eng=G)
            k = b.free = tt(bv(ro[:, 0:256 * rope]), bv(b.ap[:, 0:256 * rope]), bc(sinT, rope, 1), MUL, k2)
            yield
            k = tt(xr, xc[:, 0:256 * rope], ro[:, 0:256 * rope], ADD, k, kg)
            hn[key] = sfree[z] = k
            yield

        def pair(i):
            def f(j, p, tok):
                t = copyA(qT[:, 4 * i + j:4 * i + j + 2, :], p, tok)
                pend_h.append(headnorm(("q", 2 * i + j // 2), f2(qT[:, 4 * i + j:4 * i + j + 2, :]), "qg", t, 2))
                return t
            return f

        pend_h = [headnorm(("k", 0), kTt[:, 0, :], "kg", [kb_, kcc], 1), headnorm(("k", 1), kTt[:, 1, :], "kg", [kb_, kcc], 1)]
        wq_ = [load(kcols(wqkv, 512 * q, 512)) for q in range(2)]
        ada_load()
        for q in range(2):
            colproj3(wq_[q], hx, th, pair(q))
            ada_load()
            if q == 0:
                for _ in range(4):
                    for g in pend_h[0:3]:
                        next(g, None)
        for n, _ in enumerate(weave(pend_h, 3)):
            if n % 2 == 0:
                next(a11, None)
        tap("qT", qT, list(hn.values()))
        all_n = list(hn.values())
        prf, ptf2, oT_tok = [None] * 4, [all_n] * 2, [None] * 8

        def head(h):
            PTb = prT[:, 1024 * (h % 2):1024 * (h % 2) + 1024].rearrange("p (j q) -> p j q", j=4)
            bs = []
            for t in range(2):
                b = bank()
                k = mm(b.ap, qT[:, h, 128 * t:128 * t + 128], kTt[:, h // 4, :], True, True, all_n, b.free)
                bs.append((b, k))
            yield
            kp = []
            for t in range(2):
                b, k = bs[t]
                n = (2 * h + t) % 4
                P_ = pr[:, 512 * n:512 * n + 512]
                sx = st[:, 8 * n:8 * n + 8]
                k = V(lambda o=sx[:, 0:1], i=b.ap: vec.tensor_reduce(o, i, AX.X, MAX), k, prf[n])
                k = ts(sx[:, 1:2], sx[:, 0:1], -SC, None, MUL, ALU.bypass)
                k = b.free = actf(P_, b.ap, ACT.Exp, k, prf[n], bias=sx[:, 1:2], scale=SC, accum=sx[:, 2:3])
                kp.append(k)
            yield
            toks = []
            for t in range(2):
                n = (2 * h + t) % 4
                P_ = pr[:, 512 * n:512 * n + 512]
                sx = st[:, 8 * n:8 * n + 8]
                k = recip(sx[:, 3:4], sx[:, 2:3], kp[t])
                k = ts(P_, P_, sx[:, 3:4], None, MUL, ALU.bypass)
                b = bank()
                for j in range(4):
                    k2 = tr(b.ap[:, 128 * j:128 * j + 128], P_[:, 128 * j:128 * j + 128], k, b.free)
                prf[n] = k2
                cp = copyA if t == 0 else copyV
                b.free = cp(PTb[:, :, 128 * t:128 * t + 128], b.ap.rearrange("p (j n) -> p j n", j=4), k2, ptf2[h % 2])
                toks.append(b.free)
            yield
            b = bank()
            for j in range(4):
                k = mm(b.ap[:, 0:256], vt[:, j, 128 * (h // 4):128 * (h // 4) + 128], PTb[:, j, :], j == 0, j == 3,
                       toks, t_vt, b.free)
            ptf2[h % 2] = k
            oT_tok[h] = b.free = copyA(oT[:, h, :], b.ap[:, 0:256], k, all_n)
            yield

        hs = [head(h) for h in range(8)]
        for n in range(11):
            if n < 8:
                next(hs[n])
            if 0 < n <= 8:
                next(hs[n - 1])
            if n < 8:
                next(hs[n])
            if n > 1 and n - 2 < 8:
                next(hs[n - 2])
            if n == 8:
                run(a11)
                wo = [load(kcols(a["attn_w_o_2"][0], 512 * q, 512)) for q in range(2)]
            next(a11, None)
        tap("oT", oT, oT_tok)
        hfree = (PE.sem, PE.count)
        t_xa = []
        ox = [split_rows(hx[0], hx[1], c, oT[:, c, :], oT_tok[c], hfree, lo_eng=G if c % 2 else None) for c in range(8)]
        for q in range(2):
            def add_o(j, p, tok, q=q):
                for i in range(2):
                    c = 4 * q + j + i
                    k = stt(xT[:, c, :], p[:, i, :], mod(1, 2, c, 0), xT[:, c, :], MUL, ADD, tok)
                    t_xa.append(k)
                return k
            colproj3(wo[q], hx, ox, add_o)
        am.close()
        tap("xa", xT, t_xa)
        tf = ffn3(1, t_xa, all_n)
        yo = yo_[:, :].rearrange("p (t d) -> p t d", t=2)
        l_out = Line("out")
        for q in range(2):
            for t in range(2):
                b = bank()
                for j in range(4):
                    c = 4 * q + j
                    k = tr(b.ap[:, 128 * j:128 * j + 128], xT[:, c, 128 * t:128 * t + 128], tf, b.free)
                cp = copyA if t == 0 else copyV
                k = b.free = cp(yo[:, t, 512 * q:512 * q + 512], b.ap, k)
                SP.dma(lambda o=out[0, 128 * t:128 * t + 128, 512 * q:512 * q + 512], i=yo[:, t, 512 * q:512 * q + 512]:
                       nc.sync.dma_start(o, i), l_out, k)
        SP.items.append(([(l_out.sem, l_out.count)], None, None, 0))
    if tapl.count:
        SP.items.append(([(tapl.sem, tapl.count)], None, None, 0))

    block = ctx.enter_context(nc.Block())

    @block.sync
    def _(eng):
        tail = [i for i in SP.items if i[1] is None]
        SP.items = [i for i in SP.items if i[1] is not None]
        SP.play(eng)
        for waits, *_ in tail:
            for s, v in waits:
                eng.wait_ge(s, v)

    @block.tensor
    def _(eng):
        PE.play(eng)

    @block.vector
    def _(eng):
        V.play(eng)

    @block.scalar
    def _(eng):
        A.play(eng)

    @block.gpsimd
    def _(eng):
        G.play(eng)

    ctx.close()


_INS = ["x", "norm1_g", "w_in", "conv_w", "gdn_a_log", "gdn_dt_bias", "gdn_norm_g", "mlstm_i_bias",
        "mlstm_f_bias", "mlstm_norm_g", "w_out", "norm2_g", "peer_wq", "peer_keys", "peer_u", "peer_v",
        "normf_g", "c_2", "ctx_2", "c_ctx_2", "ada_w_2", "ada_b_2", "norm_w_2", "pool_w_2", "pool_b_2",
        "pool_scale_2", "attn_w_qkv_2", "attn_q_gain_2", "attn_k_gain_2", "attn_w_o_2", "ffn_w_up_2",
        "ffn_conv_w_2", "ffn_conv_b_2", "ffn_w_down_2"]


def kernel(**inputs):
    import numpy as _np
    import concourse.bacc as _bacc
    from concourse import mybir as _mybir
    from concourse.bass_utils import run_bass_kernel_spmd as _run

    nc = _bacc.Bacc("TRN2", target_bir_lowering=False, num_devices=1)
    arrays, args = {}, {}
    base, levels, late = shape_constants()
    given = {n: inputs[n] for n in _INS} | {"c_base": base, "c_levels": levels, "c_late": late}
    for name, value in given.items():
        v = _np.ascontiguousarray(value)
        arrays[f"in_{name}"] = v
        args[name] = nc.dram_tensor(f"in_{name}", v.shape, _mybir.dt.from_np(v.dtype), kind="ExternalInput").ap()
    out = nc.dram_tensor("out_0", (1, 256, 1024), _mybir.dt.float32, kind="ExternalOutput").ap()
    program(nc, args, out)
    r = _run(nc, [arrays], core_ids=[0])
    return r.results[0]["out_0"]
```
